# Optimizing a Trainium2 kernel written in Bass

```python
import math
import jax, jax.numpy as jnp
from jax import lax
import numpy as np

D_MODEL = 1024
BATCH = 1
SEQ = 512
DEPTH = 1
DEC_BATCH = 8
DEC_SEQ = 4
PAST_LEN = 1024
PAGE_SIZE = 128

D_CONV = D_MODEL // 2
CONV_W = 31
N_HEADS = 16
HEAD_DIM = D_MODEL // N_HEADS
N_KV_HEADS = 4
KV_GROUP = N_HEADS // N_KV_HEADS
IDX_HEADS = 8
IDX_DIM = 64
TOPK_MAX = 256
Q_BLOCK = 128
ROPE_THETA = 500000.0
ROPE_FRAC = 4
PEER_HEADS = 8
PEER_NKEYS = 128
PEER_N_EXPERTS = PEER_NKEYS * PEER_NKEYS
PEER_DQ = 128
PEER_TOPK = 16
PEER_BLOCK = 128
ALPHA = (2.0 * DEPTH) ** 0.25
BETA = (8.0 * DEPTH) ** -0.25
LN_EPS = 1e-5

kernel_name = 'gated_conformer_dsa_peer_decoder_step'

def _proj_layout():
    sizes = (2 * D_CONV, N_HEADS * HEAD_DIM, N_KV_HEADS * HEAD_DIM, N_KV_HEADS * HEAD_DIM,
             IDX_HEADS * IDX_DIM, IDX_DIM, IDX_HEADS, D_MODEL, D_MODEL)
    pts, acc = [], 0
    for s in sizes[:-1]:
        acc += s
        pts.append(acc)
    return sizes, pts

def layer_norm(x, g, b):
    xf = x.astype(jnp.float32)
    mu = jnp.mean(xf, axis=-1, keepdims=True)
    var = jnp.mean(jnp.square(xf - mu), axis=-1, keepdims=True)
    return ((xf - mu) * lax.rsqrt(var + LN_EPS) * g + b).astype(x.dtype)

def partial_rope(x, pos):
    d = x.shape[-1]
    r = d // ROPE_FRAC
    half = r // 2
    inv = jnp.power(ROPE_THETA, -jnp.arange(half, dtype=jnp.float32) / half)
    ang = pos.astype(jnp.float32)[:, None] * inv
    cos = jnp.cos(ang)[:, None, :]
    sin = jnp.sin(ang)[:, None, :]
    x1 = x[..., :half].astype(jnp.float32)
    x2 = x[..., half:r].astype(jnp.float32)
    rot = jnp.concatenate([x1 * cos - x2 * sin, x2 * cos + x1 * sin], axis=-1)
    return jnp.concatenate([rot.astype(x.dtype), x[..., r:]], axis=-1)

def glu(z):
    a, b = jnp.split(z, 2, axis=-1)
    return a * jax.nn.sigmoid(b)

def project_inputs(x, pos, w_in):
    N, T, _ = x.shape
    _, pts = _proj_layout()
    z = jnp.einsum('ntd,dc->ntc', x, w_in)
    glu_in, q, k, v, qi, ki, wi, g_conv, g_attn = jnp.split(z, pts, axis=-1)
    u = glu(glu_in)
    q = partial_rope(q.reshape(N, T, N_HEADS, HEAD_DIM), pos)
    k = partial_rope(k.reshape(N, T, N_KV_HEADS, HEAD_DIM), pos)
    v = v.reshape(N, T, N_KV_HEADS, HEAD_DIM)
    qi = partial_rope(qi.reshape(N, T, IDX_HEADS, IDX_DIM), pos)
    ki = partial_rope(ki[:, :, None, :], pos)[:, :, 0, :]
    return u, q, k, v, qi, ki, wi, g_conv, g_attn

def conformer_conv(u, prev, conv_w, conv_b, conv_ln_g, conv_ln_b, w_conv_out):
    full = jnp.concatenate([prev, u], axis=1)
    y = lax.conv_general_dilated(full, conv_w[:, None, :], window_strides=(1,), padding='VALID',
                                 dimension_numbers=('NWC', 'WIO', 'NWC'),
                                 feature_group_count=D_CONV) + conv_b
    y = jax.nn.silu(layer_norm(y, conv_ln_g, conv_ln_b))
    out = jnp.einsum('ntc,cd->ntd', y, w_conv_out)
    return out, full[:, -(CONV_W - 1):]

def indexer_scores(qi, wi, ki):
    s = jax.nn.relu(jnp.einsum('nqhd,nld->nqhl', qi, ki).astype(jnp.float32))
    w = wi.astype(jnp.float32) * (IDX_HEADS * IDX_DIM) ** -0.5
    return jnp.einsum('nqh,nqhl->nql', w, s)

def select_keys(score, qpos, topk):
    kpos = jnp.arange(score.shape[-1], dtype=jnp.int32)
    adm = kpos[None, None, :] <= qpos[None, :, None]
    top_s, idx = lax.top_k(jnp.where(adm, score, -jnp.inf), topk)
    return idx, jnp.isfinite(top_s)

def sparse_attend(q, ks, vs, valid):
    N, tq = q.shape[:2]
    qg = q.reshape(N, tq, N_KV_HEADS, KV_GROUP, HEAD_DIM)
    s = jnp.einsum('nqhgd,nqkhd->nqhgk', qg, ks).astype(jnp.float32) * HEAD_DIM ** -0.5
    s = jnp.where(valid[:, :, None, None, :], s, -jnp.inf)
    p = jax.nn.softmax(s, axis=-1)
    o = jnp.einsum('nqhgk,nqkhd->nqhgd', p.astype(vs.dtype), vs)
    return o.reshape(N, tq, N_HEADS * HEAD_DIM)

_gather_rows = jax.vmap(lambda a, i: jnp.take(a, i, axis=0))

def attn_prompt(q, k, v, qi, ki, wi):
    N, T = q.shape[:2]
    topk = min(TOPK_MAX, T // 4)
    nb = T // Q_BLOCK
    pos = jnp.arange(T, dtype=jnp.int32)

    def blocks(a):
        return a.reshape((N, nb, Q_BLOCK) + a.shape[2:]).swapaxes(0, 1)

    def body(xs):
        qb, qib, wib, pb = xs
        idx, valid = select_keys(indexer_scores(qib, wib, ki), pb, topk)
        return sparse_attend(qb, _gather_rows(k, idx), _gather_rows(v, idx), valid)

    o = lax.map(body, (blocks(q), blocks(qi), blocks(wi), pos.reshape(nb, Q_BLOCK)))
    return o.swapaxes(0, 1).reshape(N, T, N_HEADS * HEAD_DIM)

def attn_sample(q, k_new, v_new, qi, ki_new, wi, cache_k, cache_v, cache_kidx, page_table):
    N, tq = q.shape[:2]
    past = page_table.shape[1] * PAGE_SIZE
    L = past + tq
    topk = min(TOPK_MAX, L // 4)
    ki_past = cache_kidx[page_table].reshape(N, past, IDX_DIM)
    ki_all = jnp.concatenate([ki_past, ki_new.astype(ki_past.dtype)], axis=1)
    qpos = past + jnp.arange(tq, dtype=jnp.int32)
    idx, valid = select_keys(indexer_scores(qi, wi, ki_all), qpos, topk)
    in_past = (idx < past)[..., None, None]
    pidx = jnp.minimum(idx, past - 1)
    n_idx = jnp.arange(N, dtype=jnp.int32)[:, None, None]
    phys = page_table[n_idx, pidx // PAGE_SIZE]
    slot = pidx % PAGE_SIZE
    nidx = jnp.clip(idx - past, 0, tq - 1)
    ks = jnp.where(in_past, cache_k[phys, slot], _gather_rows(k_new, nidx))
    vs = jnp.where(in_past, cache_v[phys, slot], _gather_rows(v_new, nidx))
    return sparse_attend(q, ks, vs, valid)

def peer_ffn(x2, peer_w_query, peer_keys1, peer_keys2, peer_u, peer_v):
    n = x2.shape[0]
    qh = jnp.einsum('nd,dhk->nhk', x2, peer_w_query)
    q1, q2 = qh[..., :PEER_DQ // 2], qh[..., PEER_DQ // 2:]
    s1 = jnp.einsum('nhk,hmk->nhm', q1, peer_keys1).astype(jnp.float32)
    s2 = jnp.einsum('nhk,hmk->nhm', q2, peer_keys2).astype(jnp.float32)
    t1, i1 = lax.top_k(s1, PEER_TOPK)
    t2, i2 = lax.top_k(s2, PEER_TOPK)
    cand = (t1[..., :, None] + t2[..., None, :]).reshape(n, PEER_HEADS, PEER_TOPK * PEER_TOPK)
    cidx = (i1[..., :, None] * PEER_NKEYS + i2[..., None, :]).reshape(n, PEER_HEADS, PEER_TOPK * PEER_TOPK)
    ts, j = lax.top_k(cand, PEER_TOPK)
    eidx = jnp.take_along_axis(cidx, j, axis=-1)
    g = jax.nn.softmax(ts, axis=-1)
    u = peer_u[eidx]
    v = peer_v[eidx]
    a = jax.nn.gelu(jnp.einsum('nd,nhed->nhe', x2, u).astype(jnp.float32), approximate=False)
    return jnp.einsum('nhe,nhed->nd', (g * a).astype(v.dtype), v)

def merge_and_channel_mix(x, conv_out, attn_out, g_conv, g_attn, w_out, ln1_g, ln1_b,
                          peer_w_query, peer_keys1, peer_keys2, peer_u, peer_v, ln2_g, ln2_b, blocked):
    m = jax.nn.sigmoid(g_conv) * conv_out + jax.nn.sigmoid(g_attn) * attn_out
    h = layer_norm(ALPHA * x + jnp.einsum('ntd,de->nte', m, w_out), ln1_g, ln1_b)
    N, T, D = h.shape
    h2 = h.reshape(N * T, D)
    fn = lambda hb: peer_ffn(hb, peer_w_query, peer_keys1, peer_keys2, peer_u, peer_v)
    if blocked:
        f = lax.map(fn, h2.reshape(-1, PEER_BLOCK, D)).reshape(N * T, D)
    else:
        f = fn(h2)
    return layer_norm(ALPHA * h + f.reshape(N, T, D), ln2_g, ln2_b)

def setup_inputs(seed: int = 0) -> dict:
    key = jax.random.key(seed)
    ks = jax.random.split(key, 24)
    n_pages = PAST_LEN // PAGE_SIZE
    n_used = DEC_BATCH * n_pages
    n_pool = n_used + max(1, n_used // 4)
    nrm = lambda k, shape: jax.random.normal(k, shape, dtype=jnp.float32)
    sizes, _ = _proj_layout()
    col_scale = jnp.concatenate([jnp.full((s,), sc, dtype=jnp.float32) for s, sc in
                                 zip(sizes, (1.0, 1.0, 1.0, BETA, 1.0, 1.0, 1.0, 1.0, 1.0))])
    page_table = jax.random.permutation(ks[0], n_pool)[:n_used].reshape(DEC_BATCH, n_pages).astype(jnp.int32)
    return {
        'x_prompt': nrm(ks[1], (BATCH, SEQ, D_MODEL)),
        'x_sample': nrm(ks[2], (DEC_BATCH, DEC_SEQ, D_MODEL)),
        'cache_k': nrm(ks[3], (n_pool, PAGE_SIZE, N_KV_HEADS, HEAD_DIM)),
        'cache_v': nrm(ks[4], (n_pool, PAGE_SIZE, N_KV_HEADS, HEAD_DIM)) * BETA,
        'cache_kidx': nrm(ks[5], (n_pool, PAGE_SIZE, IDX_DIM)),
        'state_conv': nrm(ks[6], (DEC_BATCH, CONV_W - 1, D_CONV)) * 0.5,
        'page_table': page_table,
        'w_in': nrm(ks[7], (D_MODEL, sum(sizes))) * D_MODEL ** -0.5 * col_scale,
        'conv_w': nrm(ks[8], (CONV_W, D_CONV)) * CONV_W ** -0.5,
        'conv_b': nrm(ks[9], (D_CONV,)) * 0.01,
        'conv_ln_g': 1.0 + 0.05 * nrm(ks[10], (D_CONV,)),
        'conv_ln_b': 0.01 * nrm(ks[11], (D_CONV,)),
        'w_conv_out': nrm(ks[12], (D_CONV, D_MODEL)) * D_CONV ** -0.5 * BETA,
        'w_out': nrm(ks[13], (D_MODEL, D_MODEL)) * D_MODEL ** -0.5 * BETA,
        'ln1_g': 1.0 + 0.05 * nrm(ks[14], (D_MODEL,)),
        'ln1_b': 0.01 * nrm(ks[15], (D_MODEL,)),
        'peer_w_query': nrm(ks[16], (D_MODEL, PEER_HEADS, PEER_DQ)) * D_MODEL ** -0.5,
        'peer_keys1': nrm(ks[17], (PEER_HEADS, PEER_NKEYS, PEER_DQ // 2)) * (PEER_DQ // 2) ** -0.5,
        'peer_keys2': nrm(ks[18], (PEER_HEADS, PEER_NKEYS, PEER_DQ // 2)) * (PEER_DQ // 2) ** -0.5,
        'peer_u': nrm(ks[19], (PEER_N_EXPERTS, D_MODEL)) * D_MODEL ** -0.5,
        'peer_v': nrm(ks[20], (PEER_N_EXPERTS, D_MODEL)) * BETA,
        'ln2_g': 1.0 + 0.05 * nrm(ks[21], (D_MODEL,)),
        'ln2_b': 0.01 * nrm(ks[22], (D_MODEL,)),
    }

def reference(x_prompt, x_sample, cache_k, cache_v, cache_kidx, state_conv, page_table,
              w_in, conv_w, conv_b, conv_ln_g, conv_ln_b, w_conv_out, w_out, ln1_g, ln1_b,
              peer_w_query, peer_keys1, peer_keys2, peer_u, peer_v, ln2_g, ln2_b):
    yp, ys = x_prompt, x_sample
    for _ in range(DEPTH):
        T = yp.shape[1]
        pos_p = jnp.arange(T, dtype=jnp.int32)
        u, q, k_p, v_p, qi, kidx_p, wi, gc, ga = project_inputs(yp, pos_p, w_in)
        prev0 = jnp.zeros((yp.shape[0], CONV_W - 1, D_CONV), u.dtype)
        conv_o, conv_p = conformer_conv(u, prev0, conv_w, conv_b, conv_ln_g, conv_ln_b, w_conv_out)
        attn_o = attn_prompt(q, k_p, v_p, qi, kidx_p, wi)
        yp = merge_and_channel_mix(yp, conv_o, attn_o, gc, ga, w_out, ln1_g, ln1_b, peer_w_query,
                                   peer_keys1, peer_keys2, peer_u, peer_v, ln2_g, ln2_b, True)
        past = page_table.shape[1] * PAGE_SIZE
        pos_s = past + jnp.arange(ys.shape[1], dtype=jnp.int32)
        u, q, k_s, v_s, qi, kidx_s, wi, gc, ga = project_inputs(ys, pos_s, w_in)
        conv_o, conv_s = conformer_conv(u, state_conv.astype(u.dtype), conv_w, conv_b, conv_ln_g,
                                        conv_ln_b, w_conv_out)
        attn_o = attn_sample(q, k_s, v_s, qi, kidx_s, wi, cache_k, cache_v, cache_kidx, page_table)
        ys = merge_and_channel_mix(ys, conv_o, attn_o, gc, ga, w_out, ln1_g, ln1_b, peer_w_query,
                                   peer_keys1, peer_keys2, peer_u, peer_v, ln2_g, ln2_b, False)
    return (yp, ys, k_p, v_p, kidx_p, conv_p, k_s, v_s, kidx_s, conv_s)


_drawn_inputs = setup_inputs


def setup_inputs(seed=0):
    import zlib

    import numpy as np

    out = dict(_drawn_inputs(seed))
    spreads = {}
    factors = {'conv_b': 4.539, 'conv_ln_b': 6.29, 'ln2_b': 5.67}
    for name, (base, spread) in spreads.items():
        noise = np.random.default_rng([zlib.crc32(name.encode()), seed]).standard_normal(out[name].shape)
        drawn = base * np.exp(spread * noise) if base else spread * noise
        out[name] = __import__('jax').numpy.asarray(drawn.astype(out[name].dtype))
    for name, factor in factors.items():
        out[name] = (out[name] * factor).astype(out[name].dtype)
    return out
```

```python
from contextlib import ExitStack

import numpy as np
import concourse.bass as bass
from concourse import mybir

F32 = mybir.dt.float32
U32 = mybir.dt.uint32
I32 = mybir.dt.int32
ALU = mybir.AluOpType
ACT = mybir.ActivationFunctionType
AX = mybir.AxisListType

P = 128
D_MODEL = 1024
SEQ = 512
N_TILES = SEQ // P
DEC_BATCH, DEC_SEQ = 8, 4
N_SAMPLE = DEC_BATCH * DEC_SEQ
N_TOKENS = SEQ + N_SAMPLE
PAST_LEN, PAGE = 1024, 128
N_PAGES = PAST_LEN // PAGE
N_POOL = 80
D_CONV, CONV_W = 512, 31
N_HEADS, HEAD_DIM, N_KV = 16, 64, 4
KV_GROUP = N_HEADS // N_KV
D_KV = N_KV * HEAD_DIM
IDX_HEADS, IDX_DIM = 8, 64
ROPE_THETA, ROPE_DIM = 500000.0, 16
TOPK_PROMPT = min(256, SEQ // 4)
L_SAMPLE = PAST_LEN + DEC_SEQ
TOPK_SAMPLE = min(256, L_SAMPLE // 4)
PEER_HEADS, PEER_NKEYS, PEER_DQ, PEER_TOPK = 8, 128, 128, 16
SLOTS = PEER_HEADS * PEER_TOPK
ALPHA = 2.0 ** 0.25
LN_EPS = 1e-5
ATT_SCALE = HEAD_DIM ** -0.5
IDX_SCALE = (IDX_HEADS * IDX_DIM) ** -0.5
KC = D_MODEL // P
CC = D_CONV // P
MASKED = -1.0e30
TAKEN = -3.0e38
TAKEN_LIMIT = -2.0e38

Z_A, Z_B = 0, D_CONV
Z_Q = Z_B + D_CONV
Z_K = Z_Q + N_HEADS * HEAD_DIM
Z_QI = Z_K + D_KV
Z_KI = Z_QI + IDX_HEADS * IDX_DIM
Z_V = Z_KI + IDX_DIM
Z_WI = Z_V + D_KV
Z_GC = Z_WI + IDX_HEADS
Z_GA = Z_GC + D_MODEL
Z_COLS = Z_GA + D_MODEL
N_ROT = (Z_V - Z_Q) // HEAD_DIM
HEAD_AT = [(2 * (i // 8) + i % 2) * KV_GROUP + i // 2 % KV_GROUP for i in range(N_HEADS)]
BLK = 512
N_BLK = Z_COLS // BLK
BLK_REST = Z_COLS - N_BLK * BLK
RING = 4
CONV_PARAMS = CONV_W + 3
QB = 2 * DEC_SEQ


def build(nc, io):
    with ExitStack() as ctx:
        _build(nc, io, ctx)


def _build(nc, io, ctx):
    class Chain:

        def __init__(self, eng, semaphore):
            self.eng, self.sem, self.n = eng, semaphore, 0

        def restart(self):
            self.until(self.n)
            self.eng.sem_clear(self.sem)
            self.n = 0

        def mark(self, ins):
            ins.then_inc(self.sem, 1)
            self.n += 1
            return self.n

        def until(self, n):
            self.eng.wait_ge(self.sem, n)

        def link(self, ins):
            self.until(self.mark(ins))

    def sb(name, cols, parts=P, dt=F32):
        return ctx.enter_context(nc.sbuf_tensor(name, [parts, cols], dt))

    w_conv_out = sb("w_conv_out_s", CC * D_MODEL)
    w_out = sb("w_out_s", KC * D_MODEL)
    w_query = sb("w_query_s", KC * D_MODEL)
    peer_keys = sb("peer_keys_s", PEER_HEADS * 2 * PEER_NKEYS)
    ident = sb("ident_s", P)
    kT = sb("kT", N_KV * SEQ)
    kiT = sb("kiT", SEQ)
    vrows = sb("vrows", N_TILES * D_KV)
    conv_p = sb("conv_p", CC * CONV_PARAMS)
    zt = sb("zt", Z_COLS)
    rope = sb("rope_s", 2 * ROPE_DIM)
    causal = sb("causal_s", SEQ)
    qT = sb("qT", N_HEADS * P)
    qiT = sb("qiT", IDX_HEADS * P)
    soft = sb("soft", 2 * SEQ + 2 * SEQ)
    score = sb("score", SEQ)
    bias = sb("bias", SEQ)
    uT = sb("uT", CC * (P + CONV_W - 1))
    conv_acc = sb("conv_acc", D_CONV)
    conv_n = sb("conv_n", D_CONV)
    xh = sb("xh", 2 * D_MODEL)
    x_t = xh[:, 0:D_MODEL]
    h_t = xh[:, D_MODEL:]
    actT = sb("actT", KC * P)
    small = sb("small", 1024)
    eidx = sb("eidx", SLOTS, dt=U32)
    gate = sb("gate", SLOTS)
    diag = sb("diag", RING * P)
    rings = sb("rings", 2 * RING * D_MODEL)
    rope_tmp = rings[:, 0:2 * N_ROT * ROPE_DIM]

    bank = [ctx.enter_context(nc.psum_tensor(f"bank{i}", [P, BLK], F32)) for i in range(4)]
    acc = ctx.enter_context(nc.psum_tensor("acc", [P, D_MODEL], F32))
    wide = ctx.enter_context(nc.psum_tensor("wide", [P, D_MODEL], F32))
    s_bank = bank[0:2]
    t_bank = bank[2:4]
    proj_bank = [*bank, acc[:, 0:BLK]]

    zs = nc.dram_tensor("z_rows", (N_TILES + 1, P, Z_COLS), F32, kind="Internal").ap()
    att_s = nc.dram_tensor("att_sample", (DEC_BATCH, P, HEAD_DIM), F32, kind="Internal").ap()
    e_s = nc.dram_tensor("e_sample", (N_SAMPLE, SLOTS), U32, kind="Internal").ap()
    g_s = nc.dram_tensor("g_sample", (N_SAMPLE, SLOTS), F32, kind="Internal").ap()
    h_s = nc.dram_tensor("h_sample", (N_SAMPLE, D_MODEL), F32, kind="Internal").ap()

    xT = zt[:, 0:KC * N_TOKENS].rearrange("p (c n) -> p c n", c=KC)
    w_ring = rings[:, :].rearrange("p (r c n) -> p r c n", r=2, c=KC)
    z_stage = qT[:, :]
    z_stage_s = qiT[:, 0:BLK]
    wco = w_conv_out[:, :].rearrange("p (c n) -> p c n", c=CC)
    wou = w_out[:, :].rearrange("p (c n) -> p c n", c=KC)
    wqu = w_query[:, :].rearrange("p (c n) -> p c n", c=KC)
    pk = peer_keys[:, :].rearrange("p (h n) -> p h n", h=PEER_HEADS)
    cp = conv_p[:, :].rearrange("p (c n) -> p c n", c=CC)
    kT3 = kT[0:HEAD_DIM, :].rearrange("p (h n) -> p h n", h=N_KV)
    v3 = vrows[:, :].rearrange("p (t n) -> p t n", t=N_TILES)
    qT3 = qT[0:HEAD_DIM, :].rearrange("p (h n) -> p h n", h=N_HEADS)
    qiT3 = qiT[0:IDX_DIM, :].rearrange("p (h n) -> p h n", h=IDX_HEADS)
    sc2 = soft[:, 0:2 * SEQ].rearrange("p (b n) -> p b n", b=2)
    pt2 = soft[:, 2 * SEQ:4 * SEQ].rearrange("p (b n) -> p b n", b=2)
    ln_gb = soft[:, :].rearrange("p (b n) -> p b n", b=2)
    uT3 = uT[:, :].rearrange("p (c n) -> p c n", c=CC)
    ca3 = conv_acc[:, :].rearrange("p (c n) -> p c n", c=CC)
    cy3 = ca3
    aT3 = actT[:, :].rearrange("p (c n) -> p c n", c=KC)
    u_ring = rings[:, 0:RING * D_MODEL].rearrange("p (r n) -> p r n", r=RING)
    v_ring = rings[:, RING * D_MODEL:].rearrange("p (r n) -> p r n", r=RING)
    dg = diag[:, :].rearrange("p (r n) -> p r n", r=RING)

    sk = zt[:, 0:2048].rearrange("p (h s n) -> p h s n", h=PEER_HEADS, s=2)
    cand = zt[:, 2048:4096].rearrange("p (h n) -> p h n", h=PEER_HEADS)
    onehot = qT[:, :].rearrange("p (x n) -> p x n", n=PEER_TOPK)
    qhT = qiT[:, :].rearrange("p (h n) -> p h n", h=PEER_HEADS)
    top_v = actT[:, 0:256].rearrange("p (h s n) -> p h s n", h=PEER_HEADS, s=2)
    top_i = actT[:, 256:512].bitcast(U32).rearrange("p (h s n) -> p h s n", h=PEER_HEADS, s=2)
    top_if = actT[:, 512:768].rearrange("p (h s n) -> p h s n", h=PEER_HEADS, s=2)
    c_val = small[:, 512:640]
    c_idx = small[:, 640:768].bitcast(U32)
    c_row = actT[:, 768:896]
    c_rowu = actT[:, 896:1024].bitcast(U32)
    iota16 = small[:, 768:784]
    quarter = small[:, 784:816]
    zero = small[:, 896:1024]
    c_e1 = conv_n[:, 0:128]
    c_e2 = conv_n[:, 128:256]
    row_max = small[:, 0:16]
    neg_max = small[:, 16:32]
    row_sum = small[:, 32:48]
    row_inv = small[:, 48:64]
    stats = small[:, 64:76]
    mean_var = small[:, 76:78]
    rstd = small[:, 78:79]
    top8 = small[:, 80:88]
    wi_s = small[:, 88:96]
    g_max = small[:, 96:104]
    g_sum = small[:, 104:112]
    g_inv = small[:, 112:120]
    a4 = [small[:, 120 + 4 * g:124 + 4 * g] for g in range(2)]
    w4 = [small[:, 128 + 4 * g:132 + 4 * g] for g in range(2)]
    ge4 = [small[:, 136 + 4 * g:140 + 4 * g] for g in range(2)]
    idx4 = [small[:, 144 + 4 * g:148 + 4 * g].bitcast(U32) for g in range(2)]
    logits = small[:, 256:384]
    key_bank = [*t_bank, *s_bank]

    def sem(name):
        return ctx.enter_context(nc.semaphore(name))

    xT_in = sem("xT_in")
    w_in = [sem("w_in0"), sem("w_in1")]
    consts_in = sem("consts_in")
    projected = sem("projected")
    z_copied = sem("z_copied")
    z_stored = [sem(f"z_stored{t}") for t in range(N_TILES + 1)]
    tile_done = sem("tile_done")
    z_loaded = sem("z_loaded")
    sig_b = sem("sig_b")
    u_ready = sem("u_ready")
    roped = sem("roped")
    rows_out = sem("rows_out")
    v_kept = sem("v_kept")
    transposed = sem("transposed")
    t_copied = sem("t_copied")
    idx_mm = sem("idx_mm")
    idx_relu = sem("idx_relu")
    idx_used = sem("idx_used")
    bias_ready = sem("bias_ready")
    qk_mm = sem("qk_mm")
    maxed = sem("maxed")
    exped = sem("exped")
    p_trans = sem("p_trans")
    p_copied = sem("p_copied")
    pv_mm = sem("pv_mm")
    att_ready = sem("att_ready")
    conv_done = sem("conv_done")
    conv_t = sem("conv_t")
    conv_normed = sem("conv_normed")
    conv_t2 = sem("conv_t2")
    conv_act = sem("conv_act")
    conv_mm = sem("conv_mm")
    gates_ready = sem("gates_ready")
    merged = sem("merged")
    m_trans = sem("m_trans")
    m_copied = sem("m_copied")
    out_mm = sem("out_mm")
    x_in = sem("x_in")
    h_ready = sem("h_ready")
    ln2_in = sem("ln2_in")
    h_trans = sem("h_trans")
    h_copied = sem("h_copied")
    pq_mm = sem("pq_mm")
    pq_copied = sem("pq_copied")
    key_mm = sem("key_mm")
    key_copied = sem("key_copied")
    logits_ready = sem("logits_ready")
    exp_ready = sem("exp_ready")
    var_ready = sem("var_ready")
    std_ready = sem("std_ready")
    routed = sem("routed")
    idx_staged = sem("idx_staged")
    u_in = [sem(f"u_in{k}") for k in range(RING)]
    v_in = [sem(f"v_in{k}") for k in range(RING)]
    dotted = sem("dotted")
    gelued = sem("gelued")
    weighted = sem("weighted")
    diag_ready = sem("diag_ready")
    summed = sem("summed")
    y_ready = sem("y_ready")
    y_out = tile_done
    dve_chain = sem("dve_chain")
    act_chain = sem("act_chain")
    passed = sem("passed")
    scratch = sem("scratch")
    scratch_in = sem("scratch_in")
    page_in = sem("page_in")
    kidx_in = [sem("kidx_in0"), sem("kidx_in1")]
    kv_in = sem("kv_in")
    s_idx_mm = sem("s_idx_mm")
    s_idx_relu = sem("s_idx_relu")
    s_idx_sum = sem("s_idx_sum")
    s_wsel = sem("s_wsel")
    s_score = sem("s_score")
    s_bias = sem("s_bias")
    s_qbd = sem("s_qbd")
    s_qk = sem("s_qk")
    s_max = sem("s_max")
    s_exp = sem("s_exp")
    s_pt = sem("s_pt")
    s_ptc = sem("s_ptc")
    s_pv = sem("s_pv")
    s_o = sem("s_o")
    s_rows = sem("s_rows")
    s_new = sem("s_new")
    s_zero = sem("s_zero")


    K_COLS = L_SAMPLE
    smp_k = rings[:, 0:2 * K_COLS].rearrange("p (j n) -> p j n", j=2)
    smp_v = rings[:, 2056:4360].rearrange("p (t n) -> p t n", t=N_PAGES + 1)
    smp_ki = [rings[0:IDX_DIM, 4360 + K_COLS * i:4360 + K_COLS * (i + 1)] for i in range(2)]
    smp_relu = rings[0:N_SAMPLE, 6416:6416 + K_COLS]
    smp_p = soft[:, 0:K_COLS]
    smp_causal = small[0:N_SAMPLE, 168:168 + DEC_SEQ]
    smp_score = xh[0:N_SAMPLE, 0:K_COLS]
    smp_qbd = xh[:, 1028:1156].rearrange("p (j n) -> p j n", j=2)
    smp_qall = xh[:, 1156:1476].rearrange("p (j h n) -> p j h n", j=2, h=KV_GROUP)
    smp_choose = xh[0:N_SAMPLE, 1476:1732]
    smp_sel = smp_choose.rearrange("p (b n) -> p b n", b=DEC_BATCH)
    smp_eb = xh[0:N_SAMPLE, 1732:1860]
    smp_wb = [xh[0:N_SAMPLE, 1860 + 32 * i:1892 + 32 * i] for i in range(2)]
    smp_qi = [xh[0:IDX_DIM, 1924 + 32 * i:1956 + 32 * i].rearrange("p (h n) -> p h n", h=IDX_HEADS)
              for i in range(2)]
    smp_wi = small[0:N_SAMPLE, 160:168]
    smp_pt = kT[:, 0:(N_PAGES + 1) * P].rearrange("p (t n) -> p t n", t=N_PAGES + 1)
    smp_knew = kT[:, 1152:1216].rearrange("p (j n) -> p j n", j=2)
    smp_e = vrows[0:N_SAMPLE, :].rearrange("p (b n) -> p b n", b=DEC_BATCH)
    smp_uT = qT[:, 0:CC * DEC_BATCH * 34].rearrange("p (c b n) -> p c b n", c=CC, b=DEC_BATCH)
    smp_uTf = qT[:, 0:CC * DEC_BATCH * 34]
    smp_o = score[:, 0:HEAD_DIM]
    smp_stat = small[:, 176:190]
    smp_acc3 = conv_acc[:, 0:CC * N_SAMPLE].rearrange("p (c b n) -> p c b n", c=CC, b=DEC_BATCH)
    smp_acc = conv_acc[:, 0:CC * N_SAMPLE].rearrange("p (c n) -> p c n", c=CC)
    page_s = ctx.enter_context(nc.sbuf_tensor("page_s", [1, DEC_BATCH * N_PAGES], I32))
    eidx4 = small[:, 192:224].bitcast(U32)
    gate4 = small[:, 224:256]

    def wait_apart(eng, semaphore, value):
        eng.wait_ge(semaphore, value)
        eng.sem_inc(passed, 1)

    S_T = N_TILES
    block = ctx.enter_context(nc.Block())
    GROUPS = 9
    k_group, ki_group, u_group = 0, 1, 8

    def proj_slot(t):
        n = P if t < N_TILES else N_SAMPLE
        return (z_stage[:, t * BLK:(t + 1) * BLK] if t < N_TILES else z_stage_s), n

    @block.sync
    def _(sp):
        sp.dma_start(xT, io["xT"]).then_inc(xT_in, 16)
        for r in range(2):
            sp.dma_start(w_ring[:, r], io["w_in"][r]).then_inc(w_in[r], 16)
        with sp.Fori(1, N_BLK // 2) as i:
            for r in range(2):
                sp.wait_ge(projected, (i * 2 + (r - 1)) * 5)
                sp.dma_start(w_ring[:, r], io["w_in"][i * 2 + r]).then_inc(w_in[r], 16)
        sp.wait_ge(projected, (N_BLK - 1) * 5)
        sp.dma_start(w_ring[:, 0, :, 0:BLK_REST], io["w_in_rest"]).then_inc(w_in[0], 16)
        for t in range(N_TILES + 1):
            sp.wait_ge(z_stored[t], 16 * (N_BLK + 2))

        def tile_loads(t, n):
            sp.wait_ge(tile_done, 16 * t + 16)
            sp.dma_start(zt[0:n, :], zs[t, 0:n, :]).then_inc(z_loaded, 16)
            sp.dma_start(rope[0:n, :], io["rope"][t, 0:n, :]).then_inc(z_loaded, 16)

        def norm_loads(t, n, x_rows):
            sp.dma_start(x_t[0:n, :], x_rows).then_inc(x_in, 16)
            sp.dma_start(ln_gb[0:n], io["ln1"].partition_broadcast(n)).then_inc(x_in, 16)
            sp.wait_ge(h_ready, t + 1)
            sp.dma_start(ln_gb[0:n], io["ln2"].partition_broadcast(n)).then_inc(ln2_in, 16)

        with sp.Fori(0, N_TILES) as t:
            tile_loads(t, P)
            sp.dma_start(causal[:, :], io["causal"][t]).then_inc(z_loaded, 16)
            sp.wait_ge(u_ready, t + 1)
            sp.dma_start(io["conv_prompt"], zt[P - (CONV_W - 1):P, Z_A:Z_A + D_CONV]).then_inc(rows_out, 16)
            sp.wait_ge(roped, t + 1)
            sp.dma_start(io["k_prompt"][t], zt[:, Z_K:Z_K + D_KV]).then_inc(rows_out, 16)
            sp.dma_start(io["v_prompt"][t], zt[:, Z_V:Z_V + D_KV]).then_inc(rows_out, 16)
            sp.dma_start(io["kidx_prompt"][t], zt[:, Z_KI:Z_KI + IDX_DIM]).then_inc(rows_out, 16)
            sp.wait_ge(pv_mm, t * N_HEADS + N_HEADS)
            norm_loads(t, P, io["x_rows"][t])
            sp.wait_ge(y_ready, t + 1)
            sp.dma_start(io["y_prompt"][t], x_t[:, :]).then_inc(tile_done, 16)

        n = N_SAMPLE
        tile_loads(S_T, n)
        sp.dma_start(page_s[:, :], io["page_table"]).then_inc(page_in, 16)
        sp.dma_start(smp_uTf, io["state_T"]).then_inc(page_in, 16)
        sp.dma_start(smp_causal, io["causal_sample"]).then_inc(z_loaded, 16)
        sp.dma_start(vrows[0:n, :], io["spread"]).then_inc(page_in, 16)
        sp.dma_start(smp_choose, io["choose"]).then_inc(page_in, 16)
        for h in range(IDX_HEADS):
            sp.dma_start(smp_wi[h * DEC_SEQ:(h + 1) * DEC_SEQ, :],
                         zs[S_T, 0:n, Z_WI + h].rearrange("(b q) -> q b", q=DEC_SEQ),
                         allow_slow_non_contiguous=True).then_inc(page_in, 16)
        sp.wait_ge(page_in, 16 * 12)

        with sp.Fori(0, DEC_BATCH // 2) as i:
            for r in range(2):
                b = i * 2 + r
                sp.wait_ge(s_idx_mm, b + 1)
                for j in range(N_PAGES):
                    page = sp.value_load(page_s[0:1, bass.ds(b * N_PAGES + j, 1)], min_val=0, max_val=N_POOL - 1)
                    sp.dma_start(smp_ki[r][:, j * PAGE:(j + 1) * PAGE], io["kidx_T"][page]).then_inc(kidx_in[r], 16)
        sp.wait_ge(u_ready, S_T + 1)
        sp.dma_start(io["conv_sample"][:, CONV_W - 1 - DEC_SEQ:, :],
                     zt[0:n, Z_A:Z_A + D_CONV]).then_inc(rows_out, 16)
        sp.dma_start(io["conv_sample"][:, 0:CONV_W - 1 - DEC_SEQ, :],
                     io["state_conv"][:, DEC_SEQ:, :]).then_inc(rows_out, 16)
        sp.wait_ge(roped, S_T + 1)
        sp.dma_start(io["k_sample"], zt[0:n, Z_K:Z_K + D_KV]).then_inc(rows_out, 16)
        sp.dma_start(io["v_sample"], zt[0:n, Z_V:Z_V + D_KV]).then_inc(rows_out, 16)
        sp.dma_start(io["kidx_sample"], zt[0:n, Z_KI:Z_KI + IDX_DIM]).then_inc(rows_out, 16)

        with sp.Fori(0, DEC_BATCH) as b:
            sp.wait_ge(s_pv, b + 1)
            for j in range(N_PAGES):
                page = sp.value_load(page_s[0:1, bass.ds(b * N_PAGES + j, 1)], min_val=0, max_val=N_POOL - 1)
                sp.dma_start(smp_k[:, :, j * PAGE:(j + 1) * PAGE],
                             io["cache_kT"][page].rearrange("p (j n) -> p j n", j=2)).then_inc(kv_in, 16)
                sp.dma_start(smp_v[:, j, :], io["cache_v"][page]).then_inc(kv_in, 16)
            sp.dma_start(smp_v[0:DEC_SEQ, N_PAGES, :],
                         zs[S_T, bass.ds(b * DEC_SEQ, DEC_SEQ), Z_V:Z_V + D_KV]).then_inc(kv_in, 16)
            sp.wait_ge(s_o, b + 2)
            sp.dma_start(att_s[b], smp_o).then_inc(s_rows, 16)
        sp.wait_ge(s_rows, 16 * DEC_BATCH + 16)
        for b in range(DEC_BATCH):
            rows = att_s[b].rearrange("(h q) d -> q h d", q=QB)[0:DEC_SEQ]
            dst = zt[b * DEC_SEQ:(b + 1) * DEC_SEQ, Z_Q:Z_Q + D_MODEL].rearrange("q (h d) -> q h d", h=N_HEADS)
            sp.dma_start(dst, rows).then_inc(scratch_in, 16)
        norm_loads(S_T, n, io["x_rows"][S_T, 0:n, :])
        sp.wait_ge(routed, S_T + 1)
        sp.dma_start(e_s, eidx[0:n, :]).then_inc(scratch, 16)
        sp.dma_start(g_s, gate[0:n, :]).then_inc(scratch, 16)
        sp.dma_start(h_s, h_t[0:n, :]).then_inc(scratch, 16)
        sp.wait_ge(scratch, 48)
        for k in range(4):
            rows, cols = slice(n * k, n * (k + 1)), slice(SLOTS // 4 * k, SLOTS // 4 * (k + 1))
            sp.dma_start(eidx4[rows, :], e_s[:, cols]).then_inc(scratch_in, 16)
            sp.dma_start(gate4[rows, :], g_s[:, cols]).then_inc(scratch_in, 16)
            sp.dma_start(zt[rows, 0:D_MODEL], h_s).then_inc(scratch_in, 16)
        sp.wait_ge(y_ready, S_T + 1)
        sp.dma_start(io["y_sample"], x_t[0:n, :]).then_inc(tile_done, 16)
        sp.wait_ge(tile_done, 16 * (N_TILES + 2))
        sp.wait_ge(rows_out, 64 * N_TILES + 80)

    @block.gpsimd
    def _(pool):
        for dst in (uT, kT, kiT, vrows):
            nc.gpsimd.memset(dst[:, :], 0.0).then_inc(s_zero, 1)
        nc.gpsimd.memset(zero, 0.0).then_inc(s_zero, 1)
        for dst, src in ((ident, "ident"), (conv_p, "conv_params"), (w_conv_out, "w_conv_out"), (w_out, "w_out"),
                         (w_query, "w_query"), (peer_keys, "peer_keys")):
            pool.dma_start(dst[:, :], io[src]).then_inc(consts_in, 16)
        pool.dma_start(iota16, io["iota16"]).then_inc(consts_in, 16)
        pool.dma_start(quarter, io["quarter"]).then_inc(consts_in, 16)

        def gathers(t, steps, rows_idx, groups):
            with pool.Fori(0, steps) as i:
                for g in range(2):
                    pool.wait_ge(dotted, t * SLOTS + i * 8 + g * 4 + 1)
                    nc.gpsimd.tensor_copy(idx4[g], rows_idx[:, bass.ds(i * 8 + g * 4, 4)]).then_inc(idx_staged, 1)
                    wait_apart(pool, idx_staged, t * (SLOTS // 4) + i * 2 + g + 1)
                    for k in range(RING):
                        offs = bass.IndirectOffsetOnAxis(ap=idx4[g][:, k:k + 1], axis=0)
                        wait_apart(pool, dotted, t * SLOTS + i * 8 + g * 4 + k + 1)
                        nc.gpsimd.indirect_dma_start(u_ring[:, k, :], None, io["peer_u"], offs).then_inc(u_in[k], 16)
                        wait_apart(pool, summed, t * SLOTS + i * 8 + g * 4 + k + 1)
                        nc.gpsimd.indirect_dma_start(v_ring[:, k, :], None, io["peer_v"], offs).then_inc(v_in[k], 16)

        with pool.Fori(0, N_TILES) as t:
            pool.wait_ge(z_loaded, 48 * t + 48)
            pool.wait_ge(s_zero, 5)
            nc.gpsimd.tensor_copy(v3[:, t, :], zt[:, Z_V:Z_V + D_KV]).then_inc(v_kept, 1)
            wait_apart(pool, routed, t + 1)
            gathers(t, SLOTS // 8, eidx, 2)
        pool.wait_ge(tile_done, 16 * N_TILES + 16)
        nc.gpsimd.memset(smp_qall, 0.0).then_inc(s_zero, 1)
        nc.gpsimd.memset(smp_qbd, 0.0).then_inc(s_zero, 1)
        pool.wait_ge(scratch_in, 16 * 20)
        gathers(S_T, SLOTS // 32, eidx4, 2)

    @block.scalar
    def _(act):
        chain = Chain(act, act_chain)
        act.sem_inc(tile_done, 16)
        act.sem_inc(z_copied, 5)
        for t in range(N_TILES + 1):
            act.sem_inc(z_stored[t], 16)

        def store_block(i, width):
            for t in range(N_TILES + 1):
                dst, n = proj_slot(t)
                act.wait_ge(projected, i * 5 + t + 1)
                act.wait_ge(z_stored[t], i * 16 + 16)
                nc.scalar.copy(dst[0:n, 0:width], proj_bank[t][0:n, 0:width]).then_inc(z_copied, 1)
                act.wait_ge(z_copied, i * 5 + t + 6)
                act.dma_start(zs[t, 0:n, bass.ds(i * BLK, width)], dst[0:n, 0:width]).then_inc(z_stored[t], 16)

        with act.Fori(0, N_BLK) as i:
            store_block(i, BLK)
        store_block(N_BLK, BLK_REST)

        def gates(t, n):
            act.wait_ge(z_loaded, 48 * t + 48)
            nc.scalar.activation(zt[0:n, Z_B:Z_B + D_CONV], zt[0:n, Z_B:Z_B + D_CONV], ACT.Sigmoid).then_inc(sig_b, 1)
            nc.scalar.activation(zt[0:n, Z_GC:], zt[0:n, Z_GC:], ACT.Sigmoid).then_inc(gates_ready, 1)

        def copy_group(g, dst, src):
            act.wait_ge(transposed, g + 1)
            nc.scalar.copy(dst, src).then_inc(t_copied, 1)

        def deviation(number, n):
            act.wait_ge(var_ready, number + 1)
            nc.scalar.activation(rstd[0:n, :], mean_var[0:n, 1:2], ACT.Sqrt).then_inc(std_ready, 1)

        def tail(t, n):
            deviation(3 * t, n)
            act.wait_ge(conv_t2, t + 1)
            for c in range(CC):
                last = nc.scalar.activation(cy3[:, c, 0:n], t_bank[1][:, c * P:c * P + n], ACT.Silu,
                                            scale=cp[:, c, CONV_W + 1:CONV_W + 2],
                                            bias=cp[:, c, CONV_W + 2:CONV_W + 3])
            last.then_inc(conv_act, 1)
            for r in range(2):
                act.wait_ge(m_trans, 2 * t + r + 1)
                nc.scalar.copy(aT3[:, 4 * r:4 * r + 4, 0:n],
                               t_bank[r][:, :].rearrange("p (c n) -> p c n", c=4)[:, :, 0:n]).then_inc(m_copied, 1)
            act.wait_ge(out_mm, t + 1)
            deviation(3 * t + 1, n)
            for r in range(2):
                act.wait_ge(h_trans, 2 * t + r + 1)
                nc.scalar.copy(aT3[:, 4 * r:4 * r + 4, 0:n],
                               t_bank[r][:, :].rearrange("p (c n) -> p c n", c=4)[:, :, 0:n]).then_inc(h_copied, 1)
            for r in range(2):
                act.wait_ge(pq_mm, 2 * t + r + 1)
                nc.scalar.copy(qhT[:, 4 * r:4 * r + 4, 0:n],
                               s_bank[r][:, :].rearrange("p (c n) -> p c n", c=4)[:, :, 0:n]).then_inc(pq_copied, 1)
            act.wait_ge(rows_out, 64 * t + 64 if n == P else 64 * t + 80)
            for j in range(4):
                act.wait_ge(key_mm, 4 * t + j + 1)
                nc.scalar.copy(zt[0:n, 512 * j:512 * j + 512], key_bank[j][0:n, :]).then_inc(key_copied, 1)
            act.wait_ge(logits_ready, t + 1)
            nc.scalar.activation(gate[0:n, :], logits[0:n, :], ACT.Exp).then_inc(exp_ready, 1)

        def expert_weights(t, steps, m, weights_id):
            with act.Fori(0, steps) as i:
                for g in range(2):
                    act.wait_ge(dotted, t * SLOTS + i * 8 + g * 4 + 4 + RING)
                    nc.scalar.activation(ge4[g], a4[g], ACT.Gelu).then_inc(gelued, 1)
                    act.wait_ge(weighted, t * (SLOTS // 4) + i * 2 + g + 1)
                    for k in range(RING):
                        act.wait_ge(summed, t * SLOTS + i * 8 + g * 4 + k + 1)
                        nc.scalar.activation(dg[:, k, 0:m], weights_id, ACT.Copy,
                                             scale=w4[g][:, k:k + 1]).then_inc(diag_ready, 1)

        act.wait_ge(consts_in, 128)
        act.wait_ge(s_zero, 5)
        with act.Fori(0, N_TILES) as t:
            gates(t, P)
            here = bass.ds(t * P, P)
            t_view = [b[:, :].rearrange("p (c n) -> p c n", c=4) for b in t_bank]
            copy_group(t * GROUPS, kT3[:, :, here], t_view[0][0:HEAD_DIM])
            copy_group(t * GROUPS + 1, kiT[0:IDX_DIM, here], t_bank[1][0:IDX_DIM, 0:P])
            for g in range(2):
                copy_group(t * GROUPS + 2 + g, qiT3[:, 4 * g:4 * g + 4, :], t_view[g % 2][0:IDX_DIM])
            for g in range(4):
                copy_group(t * GROUPS + 4 + g, qT3[:, 4 * g:4 * g + 4, :], t_view[g % 2][0:HEAD_DIM])
            chain.link(nc.scalar.copy(uT3[:, :, 0:CONV_W - 1], uT3[:, :, P:P + CONV_W - 1]))
            chain.restart()
            copy_group(t * GROUPS + 8, uT3[:, :, CONV_W - 1:], t_view[0])
            for h in range(IDX_HEADS):
                act.wait_ge(idx_mm, t * IDX_HEADS + h + 1)
                if h >= 2:
                    act.wait_ge(idx_used, t * IDX_HEADS + h - 1)
                nc.scalar.activation(sc2[:, h % 2, :], s_bank[h % 2][:, :], ACT.Relu).then_inc(idx_relu, 1)

            def exp(h):
                act.wait_ge(maxed, t * N_HEADS + h + 1)
                nc.scalar.activation(sc2[:, h % 2, :], sc2[:, h % 2, :], ACT.Exp, bias=neg_max[:, h:h + 1],
                                     scale=ATT_SCALE, accum_out=row_sum[:, HEAD_AT[h]:HEAD_AT[h] + 1]).then_inc(exped, 1)

            exp(0)
            for h in range(N_HEADS):
                if h + 1 < N_HEADS:
                    exp(h + 1)
                act.wait_ge(p_trans, t * N_HEADS + h + 1)
                if h >= 2:
                    act.wait_ge(pv_mm, t * N_HEADS + h - 1)
                nc.scalar.copy(pt2[:, h % 2, :], t_bank[h % 2][:, :]).then_inc(p_copied, 1)
            tail(t, P)
            expert_weights(t, SLOTS // 8, P, ident[:, :])
            deviation(3 * t + 2, P)

        n = N_SAMPLE
        gates(S_T, n)
        act.wait_ge(page_in, 16 * 12)
        base = N_TILES * GROUPS
        copy_group(base, smp_knew, t_bank[0][:, 0:2 * n].rearrange("p (j n) -> p j n", j=2))
        copy_group(base + 1, kiT[0:IDX_DIM, 0:n], t_bank[1][0:IDX_DIM, 0:n])
        copy_group(base + 2, qiT[0:IDX_DIM, 0:IDX_HEADS * n], t_bank[0][0:IDX_DIM, 0:IDX_HEADS * n])
        act.wait_ge(s_zero, 7)
        copy_group(base + 3, smp_qall[:, :, :, 0:n],
                   t_bank[1][:, 0:8 * n].rearrange("p (j h n) -> p j h n", j=2, h=KV_GROUP))
        act.wait_ge(transposed, base + 5)
        for c in range(CC):
            last = nc.scalar.copy(smp_uT[:, c, :, CONV_W - 1:],
                                  t_bank[0][:, c * n:(c + 1) * n].rearrange("p (b q) -> p b q", b=DEC_BATCH))
        last.then_inc(t_copied, 1)
        act.wait_ge(t_copied, base + 5)
        act.sem_inc(s_idx_mm, 2)
        act.sem_inc(s_idx_sum, 2)
        act.sem_inc(s_pv, 1)
        act.sem_inc(s_idx_relu, 1)
        act.sem_inc(s_o, 1)
        act.sem_inc(s_rows, 16)
        qi_all = qiT[0:IDX_DIM, 0:IDX_HEADS * n].rearrange("p (h n) -> p h n", h=IDX_HEADS)
        with act.Fori(0, DEC_BATCH // 2) as i:
            for r in range(2):
                b = i * 2 + r
                act.wait_ge(s_idx_mm, b + 1)
                nc.scalar.copy(smp_ki[r][:, PAST_LEN:], kiT[0:IDX_DIM, bass.ds(b * DEC_SEQ, DEC_SEQ)])
                nc.scalar.copy(smp_qi[r], qi_all[:, :, bass.ds(b * DEC_SEQ, DEC_SEQ)]).then_inc(s_new, 1)
                act.wait_ge(s_idx_mm, b + 3)
                act.wait_ge(s_idx_sum, b + 2)
                nc.scalar.activation(smp_relu[:, 0:BLK], s_bank[0][0:n, :], ACT.Relu)
                nc.scalar.activation(smp_relu[:, BLK:2 * BLK], s_bank[1][0:n, :], ACT.Relu)
                nc.scalar.activation(smp_relu[:, 2 * BLK:], t_bank[0][0:n, 0:DEC_SEQ],
                                     ACT.Relu).then_inc(s_idx_relu, 1)
        with act.Fori(0, DEC_BATCH) as b:
            act.wait_ge(s_pv, b + 1)
            for half in range(2):
                rows = slice(HEAD_DIM * half, HEAD_DIM * (half + 1))
                nc.scalar.copy(smp_qbd[rows, :, 32 * half:32 * half + 32].rearrange("p j (h q) -> p j h q", q=QB),
                               smp_qall[rows, :, :, bass.ds(b * DEC_SEQ, QB)])
            nc.scalar.copy(smp_eb, smp_e[:, b, :])
            nc.scalar.copy(smp_k[:, :, PAST_LEN:], smp_knew[:, :, bass.ds(b * DEC_SEQ, DEC_SEQ)]).then_inc(s_qbd, 1)
            act.wait_ge(s_max, b + 1)
            pieces = ((s_bank[0][:, :], 0), (s_bank[1][:, :], BLK), (t_bank[0][:, 0:DEC_SEQ], 2 * BLK))
            for j, (src, col) in enumerate(pieces):
                last = nc.scalar.activation(smp_p[:, col:col + src.shape[1]], src, ACT.Exp, bias=smp_stat[:, 4:5],
                                            scale=ATT_SCALE, accum_out=smp_stat[:, 5 + j:6 + j])
            last.then_inc(s_exp, 1)
            for j, (src, lo, hi) in enumerate(((t_bank[1], 0, 4), (wide[:, 0:BLK], 4, 8))):
                act.wait_ge(s_pt, b * 3 + j + 1)
                nc.scalar.copy(smp_pt[:, lo:hi, :], src[:, :].rearrange("p (t n) -> p t n", t=4)).then_inc(s_ptc, 1)
            act.wait_ge(s_pt, b * 3 + 3)
            nc.scalar.copy(smp_pt[0:DEC_SEQ, 8, :], wide[0:DEC_SEQ, BLK:BLK + P]).then_inc(s_ptc, 1)
        tail(S_T, n)
        expert_weights(S_T, SLOTS // 32, n, quarter)
        deviation(3 * S_T + 2, n)

    @block.tensor
    def _(pe):
        def project(r, i, width):
            for t in range(N_TILES + 1):
                n = P if t < N_TILES else N_SAMPLE
                pe.wait_ge(z_copied, i * 5 + t + 1)
                for c in range(KC):
                    last = nc.tensor.matmul(proj_bank[t][0:n, 0:width], xT[:, c, t * P:t * P + n],
                                            w_ring[:, r, c, 0:width], start=(c == 0), stop=(c == KC - 1))
                last.then_inc(projected, 1)

        pe.wait_ge(xT_in, 16)
        with pe.Fori(0, N_BLK // 2) as j:
            for r in range(2):
                pe.wait_ge(w_in[r], j * 16 + 16)
                project(r, j * 2 + r, BLK)
        pe.wait_ge(w_in[0], 16 * (N_BLK // 2) + 16)
        project(0, N_BLK, BLK_REST)

        def transpose_group(g, dst, parts, n, width):
            for i, part in enumerate(parts):
                last = nc.tensor.transpose(dst[0:width, i * n:(i + 1) * n], part, ident[0:n, 0:n])
            last.then_inc(transposed, 1)

        def product(dst, n, lhs, rhs, chunks):
            for half in range(2):
                for c in range(chunks):
                    last = nc.tensor.matmul(dst[0:n, half * BLK:(half + 1) * BLK], lhs[:, c, 0:n],
                                            rhs[:, c, half * BLK:(half + 1) * BLK], start=(c == 0),
                                            stop=(c == chunks - 1))
            return last

        def halves(src, n, done):
            for r in range(2):
                for c in range(4):
                    last = nc.tensor.transpose(t_bank[r][:, c * P:c * P + n], src[0:n, (4 * r + c) * P:(4 * r + c + 1) * P],
                                               ident[0:n, 0:n])
                last.then_inc(done, 1)

        def tail(t, n):
            pe.wait_ge(conv_done, t + 1)
            for c in range(CC):
                last = nc.tensor.transpose(t_bank[0][0:n, c * P:(c + 1) * P],
                                           ca3[:, c, :] if n == P else smp_acc[:, c, :], ident[:, :])
            last.then_inc(conv_t, 1)
            pe.wait_ge(conv_normed, t + 1)
            for c in range(CC):
                last = nc.tensor.transpose(t_bank[1][:, c * P:c * P + n], conv_n[0:n, c * P:(c + 1) * P],
                                           ident[0:n, 0:n])
            last.then_inc(conv_t2, 1)
            pe.wait_ge(conv_act, t + 1)
            pe.wait_ge(att_ready, t + 1)
            product(wide, n, cy3, wco, CC).then_inc(conv_mm, 1)
            pe.wait_ge(merged, t + 1)
            halves(zt[:, Z_GC:Z_GC + D_MODEL], n, m_trans)
            pe.wait_ge(m_copied, 2 * t + 2)
            product(wide, n, aT3, wou, KC).then_inc(out_mm, 1)
            pe.wait_ge(h_ready, t + 1)
            halves(h_t, n, h_trans)
            pe.wait_ge(h_copied, 2 * t + 2)
            for r in range(2):
                for h in range(4):
                    for c in range(KC):
                        col = (4 * r + h) * PEER_DQ
                        last = nc.tensor.matmul(s_bank[r][:, h * P:h * P + n], wqu[:, c, col:col + PEER_DQ],
                                                aT3[:, c, 0:n], start=(c == 0), stop=(c == KC - 1))
                last.then_inc(pq_mm, 1)
            pe.wait_ge(pq_copied, 2 * t + 2)
            for j in range(4):
                for i in range(2):
                    last = nc.tensor.matmul(key_bank[j][0:n, i * 256:(i + 1) * 256], qhT[:, 2 * j + i, 0:n],
                                            pk[:, 2 * j + i, :], start=True, stop=True)
                last.then_inc(key_mm, 1)

        def experts(t, steps, m):
            pe.wait_ge(routed, t + 1)
            for half in range(2):
                nc.tensor.matmul(acc[0:m, half * BLK:(half + 1) * BLK], zero[:, 0:m], wou[:, half, 0:BLK],
                                 start=True, stop=False, skip_group_check=True)
            with pe.Fori(0, steps) as i:
                for g in range(2):
                    for k in range(RING):
                        pe.wait_ge(v_in[k], t * (16 * SLOTS // RING) + (i * 2 + g) * 16 + 16)
                        pe.wait_ge(diag_ready, t * SLOTS + i * 8 + g * 4 + k + 1)
                        for half in range(2):
                            last = nc.tensor.matmul(acc[0:m, half * BLK:(half + 1) * BLK], dg[:, k, 0:m],
                                                    v_ring[:, k, half * BLK:(half + 1) * BLK], start=False,
                                                    stop=False, skip_group_check=True)
                        last.then_inc(summed, 1)

        pe.sem_inc(summed, RING)
        pe.wait_ge(consts_in, 128)
        pe.wait_ge(s_zero, 5)
        with pe.Fori(0, N_TILES) as t:
            here = t * GROUPS
            wait_apart(pe, roped, t + 1)
            heads = lambda col, k: [zt[:, col + HEAD_DIM * (4 * k + i):col + HEAD_DIM * (4 * k + i + 1)] for i in range(4)]
            transpose_group(0, t_bank[0], heads(Z_K, 0), P, HEAD_DIM)
            transpose_group(1, t_bank[1], [zt[:, Z_KI:Z_KI + IDX_DIM]], P, IDX_DIM)
            for g in range(2):
                wait_apart(pe, t_copied, here + 1 + g)
                transpose_group(2 + g, t_bank[g % 2], heads(Z_QI, g), P, IDX_DIM)
            for g in range(4):
                wait_apart(pe, t_copied, here + 3 + g)
                transpose_group(4 + g, t_bank[g % 2], heads(Z_Q, g), P, HEAD_DIM)
            pe.wait_ge(t_copied, here + 7)
            transpose_group(8, t_bank[0], [zt[:, Z_A + P * c:Z_A + P * (c + 1)] for c in range(CC)], P, P)
            for h in range(IDX_HEADS):
                if h >= 2:
                    pe.wait_ge(idx_relu, t * IDX_HEADS + h - 1)
                nc.tensor.matmul(s_bank[h % 2][:, :], qiT3[:, h, :], kiT[0:IDX_DIM, :], start=True,
                                 stop=True).then_inc(idx_mm, 1)
            pe.wait_ge(t_copied, here + 9)
            pe.wait_ge(idx_relu, t * IDX_HEADS + IDX_HEADS)

            def scores(h):
                if h >= 2:
                    pe.wait_ge(maxed, t * N_HEADS + h - 1)
                nc.tensor.matmul(s_bank[h % 2][:, :], qT3[:, h, :], kT3[:, HEAD_AT[h] // KV_GROUP, :], start=True,
                                 stop=True).then_inc(qk_mm, 1)

            scores(0)
            scores(1)
            pe.wait_ge(v_kept, t + 1)
            for h in range(N_HEADS):
                pe.wait_ge(exped, t * N_HEADS + h + 1)
                if h >= 2:
                    pe.wait_ge(p_copied, t * N_HEADS + h - 1)
                for j in range(N_TILES):
                    last = nc.tensor.transpose(t_bank[h % 2][:, j * P:(j + 1) * P], sc2[:, h % 2, j * P:(j + 1) * P],
                                               ident[:, :])
                last.then_inc(p_trans, 1)
                if h + 2 < N_HEADS:
                    scores(h + 2)
                pe.wait_ge(p_copied, t * N_HEADS + h + 1)
                for j in range(N_TILES):
                    o, g = HEAD_AT[h], HEAD_AT[h] // KV_GROUP
                    last = nc.tensor.matmul(wide[:, o * HEAD_DIM:(o + 1) * HEAD_DIM], pt2[:, h % 2, j * P:(j + 1) * P],
                                            v3[:, j, g * HEAD_DIM:(g + 1) * HEAD_DIM], start=(j == 0),
                                            stop=(j == N_TILES - 1))
                last.then_inc(pv_mm, 1)
            tail(t, P)
            experts(t, SLOTS // 8, P)

        n = N_SAMPLE
        base = N_TILES * GROUPS
        pe.wait_ge(roped, S_T + 1)
        transpose_group(0, t_bank[0], [zt[0:n, Z_K + P * j:Z_K + P * (j + 1)] for j in range(2)], n, P)
        transpose_group(1, t_bank[1], [zt[0:n, Z_KI:Z_KI + IDX_DIM]], n, IDX_DIM)
        pe.wait_ge(t_copied, base + 1)
        transpose_group(2, t_bank[0], [zt[0:n, Z_QI + IDX_DIM * h:Z_QI + IDX_DIM * (h + 1)] for h in range(IDX_HEADS)],
                        n, IDX_DIM)
        pe.wait_ge(t_copied, base + 2)
        transpose_group(3, t_bank[1], [zt[0:n, Z_Q + P * j:Z_Q + P * (j + 1)] for j in range(8)], n, P)
        pe.wait_ge(t_copied, base + 3)
        transpose_group(4, t_bank[0], [zt[0:n, Z_A + P * c:Z_A + P * (c + 1)] for c in range(CC)], n, P)
        pe.wait_ge(t_copied, base + 5)
        spans = ((s_bank[0], wide[:, 0:BLK], 0, BLK), (s_bank[1], wide[:, BLK:], BLK, BLK),
                 (t_bank[0], t_bank[1], 2 * BLK, DEC_SEQ))
        for _, dst, col, width in spans:
            start_from = (zero[0:n, 0:n], wou[0:n, 0, 0:BLK]) if width == BLK else (ident[0:n, 0:n], smp_causal)
            nc.tensor.matmul(dst[0:n, 0:width], *start_from, start=True, stop=False, skip_group_check=True)
        with pe.Fori(0, DEC_BATCH // 2) as i:
            for r in range(2):
                b = i * 2 + r
                pe.wait_ge(s_idx_relu, b + 1)
                pe.wait_ge(kidx_in[r], 128 * i + 128)
                wait_apart(pe, s_new, b + 1)
                for src, _, col, width in spans:
                    last = nc.tensor.matmul(src[0:n, 0:width], smp_qi[r].rearrange("p h q -> p (h q)"),
                                            smp_ki[r][:, col:col + width], start=True, stop=True)
                last.then_inc(s_idx_mm, 1)
                pe.wait_ge(s_idx_relu, b + 2)
                wait_apart(pe, s_wsel, b + 1)
                for _, dst, col, width in spans:
                    last = nc.tensor.matmul(dst[0:n, 0:width], smp_wb[r], smp_relu[:, col:col + width], start=False,
                                            stop=False, skip_group_check=True)
                last.then_inc(s_idx_sum, 1)
        with pe.Fori(0, DEC_BATCH) as b:
            pe.wait_ge(s_bias, 1)
            pe.wait_ge(kv_in, 272 * b + 272)
            pe.wait_ge(s_qbd, b + 1)
            for dst, _, col, width in spans:
                nc.tensor.matmul(dst[:, 0:width], smp_eb, smp_score[:, col:col + width], start=True, stop=False,
                                 skip_group_check=True)
                for j in range(2):
                    last = nc.tensor.matmul(dst[64 * j:64 * j + 64, 0:width], smp_qbd[:, j, :],
                                            smp_k[:, j, col:col + width], start=False, stop=(j == 1),
                                            skip_group_check=True)
            last.then_inc(s_qk, 1)
            pe.wait_ge(s_exp, b + 1)
            for dst, lo in ((t_bank[1], 0), (wide, 4)):
                for j in range(4):
                    last = nc.tensor.transpose(dst[:, j * P:(j + 1) * P], smp_p[:, (lo + j) * P:(lo + j + 1) * P],
                                               ident[:, :])
                last.then_inc(s_pt, 1)
            nc.tensor.transpose(wide[0:DEC_SEQ, BLK:BLK + P], smp_p[:, PAST_LEN:], ident[:, :]).then_inc(s_pt, 1)
            pe.wait_ge(s_ptc, b * 3 + 3)
            pe.wait_ge(s_o, b + 1)
            for j in range(N_PAGES + 1):
                rows = P if j < N_PAGES else DEC_SEQ
                last = nc.tensor.matmul(acc[:, 0:D_KV], smp_pt[0:rows, j, :], smp_v[0:rows, j, :], start=(j == 0),
                                        stop=(j == N_PAGES))
            last.then_inc(s_pv, 1)
        tail(S_T, n)
        pe.wait_ge(scratch_in, 16 * 20)
        experts(S_T, SLOTS // 32, n)

    @block.vector
    def _(dve):
        chain = Chain(dve, dve_chain)
        V = nc.vector

        def rotate(t, n):
            dve.wait_ge(z_loaded, 48 * t + 48)
            dve.wait_ge(sig_b, t + 1)
            V.tensor_tensor(zt[0:n, Z_A:Z_A + D_CONV], zt[0:n, Z_A:Z_A + D_CONV], zt[0:n, Z_B:Z_B + D_CONV],
                            ALU.mult).then_inc(u_ready, 1)
            x = zt[0:n, Z_Q:Z_V].rearrange("p (h d) -> p h d", d=HEAD_DIM)[:, :, 0:ROPE_DIM]
            half = ROPE_DIM // 2
            with_cos = rope_tmp[0:n, 0:N_ROT * ROPE_DIM].rearrange("p (h d) -> p h d", d=ROPE_DIM)
            with_sin = rope_tmp[0:n, N_ROT * ROPE_DIM:].rearrange("p (h d) -> p h d", d=ROPE_DIM)
            cos = rope[0:n, 0:ROPE_DIM].unsqueeze(1).to_broadcast([n, N_ROT, ROPE_DIM])
            sin = [rope[0:n, ROPE_DIM + half * k:ROPE_DIM + half * (k + 1)].unsqueeze(1).to_broadcast([n, N_ROT, half])
                   for k in range(2)]
            V.tensor_tensor(with_cos, x, cos, ALU.mult)
            V.tensor_tensor(with_sin[:, :, 0:half], x[:, :, half:], sin[0], ALU.mult)
            chain.link(V.tensor_tensor(with_sin[:, :, half:], x[:, :, 0:half], sin[1], ALU.mult))
            V.tensor_tensor(x, with_cos, with_sin, ALU.add).then_inc(roped, 1)

        def take_top(values, rounds):
            top = top8[0:values.shape[0], :]
            for _ in range(rounds):
                chain.link(V.max(top, values))
                chain.link(V.match_replace(values, top, values, TAKEN))

        def norm(dst, src, n, width, number):
            k = width // BLK
            for i in range(k):
                m = chain.mark(V.bn_stats(stats[0:n, 6 * i:6 * i + 6], src[0:n, i * BLK:(i + 1) * BLK]))
            chain.until(m)
            chain.link(V.bn_aggr(mean_var[0:n, :], stats[0:n, 0:6 * k]))
            V.tensor_scalar(mean_var[0:n, 1:2], mean_var[0:n, 1:2], LN_EPS, None, ALU.add).then_inc(var_ready, 1)
            dve.wait_ge(std_ready, number + 1)
            chain.link(V.reciprocal(rstd[0:n, :], rstd[0:n, :]))
            return V.tensor_scalar(dst[0:n, :], src[0:n, 0:width], mean_var[0:n, 0:1], rstd[0:n, :], ALU.subtract,
                                   ALU.mult)

        def tail(t, n):
            dve.wait_ge(conv_t, t + 1)
            norm(conv_n, t_bank[0], n, D_CONV, 3 * t).then_inc(conv_normed, 1)
            dve.wait_ge(gates_ready, t + 1)
            dve.wait_ge(conv_mm, t + 1)
            att, gc, ga = (zt[0:n, z:z + D_MODEL] for z in (Z_Q, Z_GC, Z_GA))
            chain.mark(V.tensor_tensor(gc, gc, wide[0:n, :], ALU.mult))
            chain.link(V.tensor_tensor(ga, ga, att, ALU.mult))
            V.tensor_tensor(gc, gc, ga, ALU.add).then_inc(merged, 1)
            dve.wait_ge(out_mm, t + 1)
            dve.wait_ge(x_in, 32 * t + 32)
            h = h_t[0:n, :]
            chain.link(V.scalar_tensor_tensor(h, x_t[0:n, :], ALPHA, wide[0:n, :], ALU.mult, ALU.add))
            chain.link(norm(h_t, h_t, n, D_MODEL, 3 * t + 1))
            chain.link(V.tensor_tensor(h, h, ln_gb[0:n, 0, :], ALU.mult))
            V.tensor_tensor(h, h, ln_gb[0:n, 1, :], ALU.add).then_inc(h_ready, 1)
            wait_apart(dve, key_copied, 4 * t + 4)
            for hd in range(PEER_HEADS):
                for side in range(2):
                    s, tv, ti = sk[0:n, hd, side, :], top_v[0:n, hd, side, :], top_i[0:n, hd, side, :]
                    chain.link(V.max(tv[:, 0:8], s))
                    chain.mark(V.max_index(ti[:, 0:8], tv[:, 0:8], s))
                    chain.link(V.match_replace(s, tv[:, 0:8], s, TAKEN))
                    chain.link(V.max(tv[:, 8:16], s))
                    m = chain.mark(V.max_index(ti[:, 8:16], tv[:, 8:16], s))
            chain.until(m)
            k2 = PEER_TOPK * PEER_TOPK
            chain.mark(V.tensor_copy(top_if[0:n], top_i[0:n]))
            chain.link(V.tensor_tensor(
                cand[0:n].rearrange("p h (i j) -> p h i j", i=PEER_TOPK),
                top_v[0:n, :, 0, :].unsqueeze(3).to_broadcast([n, PEER_HEADS, PEER_TOPK, PEER_TOPK]),
                top_v[0:n, :, 1, :].unsqueeze(2).to_broadcast([n, PEER_HEADS, PEER_TOPK, PEER_TOPK]), ALU.add))
            for hd in range(PEER_HEADS):
                s, lo = cand[0:n, hd, :], PEER_TOPK * hd
                chain.link(V.max(c_val[0:n, lo:lo + 8], s))
                chain.mark(V.max_index(c_idx[0:n, lo:lo + 8], c_val[0:n, lo:lo + 8], s))
                chain.link(V.match_replace(s, c_val[0:n, lo:lo + 8], s, TAKEN))
                chain.link(V.max(c_val[0:n, lo + 8:lo + 16], s))
                m = chain.mark(V.max_index(c_idx[0:n, lo + 8:lo + 16], c_val[0:n, lo + 8:lo + 16], s))
            chain.until(m)
            val3 = c_val[0:n, :].rearrange("p (h k) -> p h k", h=PEER_HEADS)
            V.tensor_tensor(logits[0:n, :].rearrange("p (h k) -> p h k", h=PEER_HEADS), val3,
                            val3[:, :, 0:1].to_broadcast([n, PEER_HEADS, PEER_TOPK]),
                            ALU.subtract).then_inc(logits_ready, 1)
            for side, found in ((0, c_e1), (1, c_e2)):
                if side == 0:
                    chain.link(V.tensor_scalar(c_rowu[0:n, :], c_idx[0:n, :], 4, None, ALU.logical_shift_right))
                else:
                    chain.link(V.tensor_scalar(c_rowu[0:n, :], c_idx[0:n, :], 15, None, ALU.bitwise_and))
                chain.link(V.tensor_copy(c_row[0:n, :], c_rowu[0:n, :]))
                chain.link(V.tensor_tensor(onehot[0:n], c_row[0:n, :].unsqueeze(2).to_broadcast([n, SLOTS, PEER_TOPK]),
                                           iota16[0:n, :].unsqueeze(1).to_broadcast([n, SLOTS, PEER_TOPK]),
                                           ALU.is_equal))
                oh4 = onehot[0:n].rearrange("p (h k) j -> p h k j", h=PEER_HEADS)
                chain.link(V.tensor_tensor(
                    oh4, oh4, top_if[0:n, :, side, :].unsqueeze(2).to_broadcast([n, PEER_HEADS, PEER_TOPK, PEER_TOPK]),
                    ALU.mult))
                chain.link(V.tensor_reduce(found[0:n, :], onehot[0:n], AX.X, ALU.add))
            chain.link(V.scalar_tensor_tensor(c_row[0:n, :], c_e1[0:n, :], float(PEER_NKEYS), c_e2[0:n, :], ALU.mult,
                                              ALU.add))
            chain.mark(V.tensor_copy(eidx[0:n, :], c_row[0:n, :]))
            dve.wait_ge(exp_ready, t + 1)
            g3 = gate[0:n, :].rearrange("p (h k) -> p h k", h=PEER_HEADS)
            chain.link(V.tensor_reduce(g_sum[0:n, :], g3, AX.X, ALU.add))
            chain.link(V.reciprocal(g_inv[0:n, :], g_sum[0:n, :]))
            V.tensor_tensor(g3, g3, g_inv[0:n, :].unsqueeze(2).to_broadcast([n, PEER_HEADS, PEER_TOPK]),
                            ALU.mult).then_inc(routed, 1)

        def expert_dots(t, steps, h_rows, gates):
            with dve.Fori(0, steps) as i:
                for g in range(2):
                    for k in range(RING):
                        dve.wait_ge(u_in[k], t * (16 * SLOTS // RING) + (i * 2 + g) * 16 + 16)
                        V.tensor_tensor_reduce(out=u_ring[:, k, :], in0=u_ring[:, k, :], in1=h_rows, scale=1.0,
                                               scalar=0.0, op0=ALU.mult, op1=ALU.add,
                                               accum_out=a4[g][:, k:k + 1]).then_inc(dotted, 1)
                    dve.wait_ge(gelued, t * (SLOTS // 4) + i * 2 + g + 1)
                    V.tensor_tensor(w4[g], ge4[g], gates[:, bass.ds(i * 8 + g * 4, 4)], ALU.mult).then_inc(weighted, 1)

        def finish(t, n, total):
            dve.wait_ge(summed, total)
            y = x_t[0:n, :]
            chain.link(V.scalar_tensor_tensor(y, h_t[0:n, :], ALPHA, acc[0:n, :], ALU.mult, ALU.add))
            chain.link(norm(x_t, x_t, n, D_MODEL, 3 * t + 2))
            dve.wait_ge(ln2_in, 16 * t + 16)
            chain.link(V.tensor_tensor(y, y, ln_gb[0:n, 0, :], ALU.mult))
            V.tensor_tensor(y, y, ln_gb[0:n, 1, :], ALU.add).then_inc(y_ready, 1)

        dve.sem_inc(dotted, RING)
        dve.wait_ge(consts_in, 128)
        with dve.Fori(0, N_TILES) as t:
            rotate(t, P)
            chain.link(V.tensor_scalar(wi_s[:, :], zt[:, Z_WI:Z_WI + IDX_HEADS], IDX_SCALE, None, ALU.mult))
            for h in range(IDX_HEADS):
                dve.wait_ge(idx_relu, t * IDX_HEADS + h + 1)
                V.scalar_tensor_tensor(score[:, :], sc2[:, h % 2, :], wi_s[:, h:h + 1],
                                       causal[:, :] if h == 0 else score[:, :], ALU.mult, ALU.add).then_inc(idx_used, 1)
                wait_apart(dve, idx_used, t * IDX_HEADS + h + 1)
            take_top(score[:, :], TOPK_PROMPT // 8)
            chain.link(V.tensor_scalar(bias[:, :], score[:, :], TAKEN_LIMIT, MASKED, ALU.is_gt, ALU.mult))
            chain.link(V.tensor_tensor(bias[:, :], bias[:, :], causal[:, :], ALU.add))

            def tap(k):
                for c in range(CC):
                    src = uT3[:, c, k:k + P]
                    if k == 0:
                        ins = V.tensor_scalar(ca3[:, c, :], src, cp[:, c, 0:1], cp[:, c, CONV_W:CONV_W + 1], ALU.mult,
                                              ALU.add)
                    else:
                        chain.until(tapped[c])
                        ins = V.scalar_tensor_tensor(ca3[:, c, :], src, cp[:, c, k:k + 1], ca3[:, c, :], ALU.mult,
                                                     ALU.add)
                    tapped[c] = chain.mark(ins)

            tapped = [0] * CC
            dve.wait_ge(t_copied, t * GROUPS + GROUPS)
            for h in range(N_HEADS):
                if h >= 2:
                    dve.wait_ge(p_trans, t * N_HEADS + h - 1)
                wait_apart(dve, qk_mm, t * N_HEADS + h + 1)
                chain.link(V.tensor_tensor_reduce(out=sc2[:, h % 2, :], in0=s_bank[h % 2][:, :], in1=bias[:, :],
                                                  scale=1.0, scalar=TAKEN, op0=ALU.add, op1=ALU.max,
                                                  accum_out=row_max[:, h:h + 1]))
                V.tensor_scalar(neg_max[:, h:h + 1], row_max[:, h:h + 1], -ATT_SCALE, None,
                                ALU.mult).then_inc(maxed, 1)
                for k in range(2 * h, min(2 * h + 2, CONV_W)):
                    tap(k)
            chain.until(max(tapped))
            V.nop().then_inc(conv_done, 1)
            dve.wait_ge(pv_mm, t * N_HEADS + N_HEADS)
            chain.link(V.reciprocal(row_inv[:, :], row_sum[:, :]))
            V.tensor_tensor(zt[:, Z_Q:Z_Q + D_MODEL].rearrange("p (h d) -> p h d", h=N_HEADS),
                            wide[:, :].rearrange("p (h d) -> p h d", h=N_HEADS),
                            row_inv[:, :].unsqueeze(2).to_broadcast([P, N_HEADS, HEAD_DIM]),
                            ALU.mult).then_inc(att_ready, 1)
            tail(t, P)
            expert_dots(t, SLOTS // 8, h_t[:, :], gate)
            finish(t, P, t * SLOTS + SLOTS + RING)
            chain.restart()

        n = N_SAMPLE
        rotate(S_T, n)
        dve.wait_ge(page_in, 16 * 12)
        dve.wait_ge(t_copied, N_TILES * GROUPS + 5)
        m = [0] * CC
        for k in range(CONV_W):
            for c in range(CC):
                src, dst = smp_uT[:, c, :, k:k + DEC_SEQ], smp_acc3[:, c]
                if k == 0:
                    ins = V.tensor_scalar(dst, src, cp[:, c, 0:1], cp[:, c, CONV_W:CONV_W + 1], ALU.mult, ALU.add)
                else:
                    chain.until(m[c])
                    ins = V.scalar_tensor_tensor(dst, src, cp[:, c, k:k + 1], dst, ALU.mult, ALU.add)
                m[c] = chain.mark(ins)
        chain.until(max(m))
        V.nop().then_inc(conv_done, 1)
        with dve.Fori(0, DEC_BATCH // 2) as i:
            for r in range(2):
                b = i * 2 + r
                dve.wait_ge(s_idx_sum, b + 1)
                V.tensor_scalar(smp_wb[r], smp_sel[:, b, :], smp_wi[:, bass.ds(b, 1)], IDX_SCALE, ALU.mult,
                                ALU.mult).then_inc(s_wsel, 1)
        dve.wait_ge(s_idx_sum, DEC_BATCH + 2)
        chain.mark(V.tensor_copy(smp_score[:, 0:2 * BLK], wide[0:n, :]))
        chain.link(V.tensor_copy(smp_score[:, 2 * BLK:], t_bank[1][0:n, 0:DEC_SEQ]))
        take_top(smp_score, TOPK_SAMPLE // 8)
        chain.link(V.tensor_scalar(smp_score, smp_score, TAKEN_LIMIT, MASKED, ALU.is_gt, ALU.mult))
        new = smp_score[:, PAST_LEN:]
        V.tensor_tensor(new, new, smp_causal, ALU.add).then_inc(s_bias, 1)
        chain.restart()
        with dve.Fori(0, DEC_BATCH) as b:
            dve.wait_ge(s_qk, b + 1)
            V.tensor_reduce(smp_stat[:, 0:1], s_bank[0][:, :], AX.X, ALU.max)
            V.tensor_reduce(smp_stat[:, 1:2], s_bank[1][:, :], AX.X, ALU.max)
            chain.link(V.tensor_reduce(smp_stat[:, 2:3], t_bank[0][:, 0:DEC_SEQ], AX.X, ALU.max))
            chain.link(V.tensor_reduce(smp_stat[:, 3:4], smp_stat[:, 0:3], AX.X, ALU.max))
            V.tensor_scalar(smp_stat[:, 4:5], smp_stat[:, 3:4], -ATT_SCALE, None, ALU.mult).then_inc(s_max, 1)
            dve.wait_ge(s_exp, b + 1)
            chain.link(V.tensor_reduce(smp_stat[:, 8:9], smp_stat[:, 5:8], AX.X, ALU.add))
            chain.link(V.reciprocal(smp_stat[:, 9:10], smp_stat[:, 8:9]))
            dve.wait_ge(s_pv, b + 2)
            dve.wait_ge(s_rows, 16 * b + 16)
            for g in range(N_KV):
                rows = slice(32 * g, 32 * g + 32)
                last = V.tensor_scalar(smp_o[rows, :], acc[rows, g * HEAD_DIM:(g + 1) * HEAD_DIM],
                                       smp_stat[rows, 9:10], None, ALU.mult)
            last.then_inc(s_o, 1)
            chain.restart()
        dve.wait_ge(scratch_in, 16 * DEC_BATCH)
        V.nop().then_inc(att_ready, 1)
        tail(S_T, n)
        dve.wait_ge(scratch_in, 16 * 20)
        expert_dots(S_T, SLOTS // 32, zt[:, 0:D_MODEL], gate4)
        finish(S_T, n, N_TILES * SLOTS + SLOTS // 4 + RING)




def _rope_tables():
    half = ROPE_DIM // 2
    inv = np.power(np.float32(ROPE_THETA), -np.arange(half, dtype=np.float32) / np.float32(half)).astype(np.float32)
    pos = np.zeros((N_TILES + 1, P), np.float32)
    pos[:N_TILES] = np.arange(SEQ).reshape(N_TILES, P)
    pos[N_TILES, :N_SAMPLE] = PAST_LEN + np.arange(N_SAMPLE) % DEC_SEQ
    angle = (pos[:, :, None] * inv).astype(np.float32)
    cos, sin = np.cos(angle), np.sin(angle)
    return np.concatenate([cos, cos, -sin, sin], -1).astype(np.float32)


def kernel(**inputs):
    import concourse.bacc as bacc
    from concourse.bass_utils import run_bass_kernel_spmd

    a = {k: np.asarray(v) for k, v in inputs.items()}
    f = np.float32

    def chunks(w):
        c = w.shape[0] // P
        return np.ascontiguousarray(w.reshape(c, P, -1).transpose(1, 0, 2).reshape(P, -1))

    x = np.zeros((N_TILES + 1, P, D_MODEL), f)
    x[:N_TILES] = a["x_prompt"].reshape(N_TILES, P, D_MODEL)
    x[N_TILES, :N_SAMPLE] = a["x_sample"].reshape(N_SAMPLE, D_MODEL)
    tokens = x.reshape(-1, D_MODEL)[:N_TOKENS]
    q0 = 2 * D_CONV
    k0 = q0 + N_HEADS * HEAD_DIM
    v0 = k0 + D_KV
    qi0 = v0 + D_KV
    ki0 = qi0 + IDX_HEADS * IDX_DIM
    wi0 = ki0 + IDX_DIM
    w = a["w_in"]
    q_cols = [w[:, q0 + h * HEAD_DIM:q0 + (h + 1) * HEAD_DIM] for h in HEAD_AT]
    w = np.concatenate([w[:, :q0], *q_cols, w[:, k0:v0], w[:, qi0:wi0], w[:, v0:qi0], w[:, wi0:]], 1)
    wb = w[:, :N_BLK * BLK].reshape(KC, P, N_BLK, BLK).transpose(2, 1, 0, 3)
    conv_params = np.concatenate([a["conv_w"], a["conv_b"][None], a["conv_ln_g"][None], a["conv_ln_b"][None]], 0).T
    keys = np.zeros((PEER_HEADS, 2, PEER_DQ // 2, 2, PEER_NKEYS), f)
    keys[:, 0, :, 0] = a["peer_keys1"].transpose(0, 2, 1)
    keys[:, 1, :, 1] = a["peer_keys2"].transpose(0, 2, 1)
    state = np.zeros((DEC_BATCH, CONV_W - 1 + DEC_SEQ, D_CONV), f)
    state[:, :CONV_W - 1] = a["state_conv"]
    query, key = np.arange(SEQ).reshape(N_TILES, P, 1), np.arange(SEQ)
    causal = np.where(key <= query, f(0), f(MASKED)).astype(f)
    n = np.arange(N_SAMPLE)
    causal_sample = np.where(np.arange(DEC_SEQ)[None] <= (n % DEC_SEQ)[:, None], f(0), f(MASKED)).astype(f)
    batch, row_q = np.arange(DEC_BATCH), np.arange(P) % QB % DEC_SEQ
    spread = (n[:, None, None] == batch[None, :, None] * DEC_SEQ + row_q[None, None, :]).astype(f)
    choose = (n[None, None, :] == batch[None, :, None] * DEC_SEQ + (n % DEC_SEQ)[:, None, None]).astype(f)
    arrays = {
        "xT": chunks(np.ascontiguousarray(tokens.T)).reshape(P, KC, N_TOKENS),
        "x_rows": x,
        "w_in": np.ascontiguousarray(wb),
        "w_in_rest": np.ascontiguousarray(w[:, N_BLK * BLK:].reshape(KC, P, -1).transpose(1, 0, 2)),
        "w_conv_out": chunks(a["w_conv_out"]),
        "w_out": chunks(a["w_out"]),
        "w_query": chunks(a["peer_w_query"].reshape(D_MODEL, -1)),
        "peer_keys": np.ascontiguousarray(keys.reshape(PEER_HEADS, P, -1).transpose(1, 0, 2).reshape(P, -1)),
        "conv_params": chunks(np.ascontiguousarray(conv_params)),
        "ln1": np.stack([a["ln1_g"], a["ln1_b"]]),
        "ln2": np.stack([a["ln2_g"], a["ln2_b"]]),
        "rope": _rope_tables(),
        "causal": causal,
        "causal_sample": causal_sample,
        "spread": np.ascontiguousarray(spread.reshape(N_SAMPLE, -1)),
        "choose": np.ascontiguousarray(choose.reshape(N_SAMPLE, -1)),
        "ident": np.eye(P, dtype=f),
        "iota16": np.tile(np.arange(PEER_TOPK, dtype=f), (P, 1)),
        "quarter": np.tile(np.eye(N_SAMPLE, dtype=f), (4, 1)),
        "page_table": a["page_table"].reshape(1, -1),
        "state_T": chunks(np.ascontiguousarray(state.transpose(2, 0, 1).reshape(D_CONV, -1))),
        "state_conv": a["state_conv"],
        "cache_kT": np.ascontiguousarray(
            a["cache_k"].reshape(N_POOL, PAGE, 2, P).transpose(0, 3, 2, 1).reshape(N_POOL, P, -1)),
        "cache_v": a["cache_v"].reshape(N_POOL, PAGE, D_KV),
        "kidx_T": np.ascontiguousarray(a["cache_kidx"].transpose(0, 2, 1)),
        "peer_u": a["peer_u"],
        "peer_v": a["peer_v"],
    }
    outputs = {
        "y_prompt": (N_TILES, P, D_MODEL),
        "y_sample": (N_SAMPLE, D_MODEL),
        "k_prompt": (N_TILES, P, D_KV),
        "v_prompt": (N_TILES, P, D_KV),
        "kidx_prompt": (N_TILES, P, IDX_DIM),
        "conv_prompt": (CONV_W - 1, D_CONV),
        "k_sample": (N_SAMPLE, D_KV),
        "v_sample": (N_SAMPLE, D_KV),
        "kidx_sample": (N_SAMPLE, IDX_DIM),
        "conv_sample": (DEC_BATCH, CONV_W - 1, D_CONV),
    }
    nc = bacc.Bacc("TRN2", target_bir_lowering=False, num_devices=1)
    io = {}
    for name, array in arrays.items():
        io[name] = nc.dram_tensor(name, array.shape, mybir.dt.from_np(array.dtype), kind="ExternalInput").ap()
    for name, shape in outputs.items():
        io[name] = nc.dram_tensor(name, shape, F32, kind="ExternalOutput").ap()
    build(nc, io)
    r = run_bass_kernel_spmd(nc, [arrays], core_ids=[0]).results[0]
    return (
        r["y_prompt"].reshape(1, SEQ, D_MODEL),
        r["y_sample"].reshape(DEC_BATCH, DEC_SEQ, D_MODEL),
        r["k_prompt"].reshape(1, SEQ, N_KV, HEAD_DIM),
        r["v_prompt"].reshape(1, SEQ, N_KV, HEAD_DIM),
        r["kidx_prompt"].reshape(1, SEQ, IDX_DIM),
        r["conv_prompt"].reshape(1, CONV_W - 1, D_CONV),
        r["k_sample"].reshape(DEC_BATCH, DEC_SEQ, N_KV, HEAD_DIM),
        r["v_sample"].reshape(DEC_BATCH, DEC_SEQ, N_KV, HEAD_DIM),
        r["kidx_sample"].reshape(DEC_BATCH, DEC_SEQ, IDX_DIM),
        r["conv_sample"],
    )
```

```python
from contextlib import ExitStack

import numpy as np
import concourse.bass as bass
from concourse import mybir

F32 = mybir.dt.float32
U32 = mybir.dt.uint32
I32 = mybir.dt.int32
ALU = mybir.AluOpType
ACT = mybir.ActivationFunctionType
AX = mybir.AxisListType

P = 128
D_MODEL = 1024
SEQ = 512
N_TILES = SEQ // P
DEC_BATCH, DEC_SEQ = 8, 4
N_SAMPLE = DEC_BATCH * DEC_SEQ
PAST_LEN, PAGE = 1024, 128
N_PAGES = PAST_LEN // PAGE
N_POOL = 80
D_CONV, CONV_W = 512, 31
N_HEADS, HEAD_DIM, N_KV = 16, 64, 4
KV_GROUP = N_HEADS // N_KV
D_KV = N_KV * HEAD_DIM
IDX_HEADS, IDX_DIM = 8, 64
ROPE_THETA, ROPE_DIM = 500000.0, 16
TOPK_PROMPT = min(256, SEQ // 4)
L_SAMPLE = PAST_LEN + DEC_SEQ
TOPK_SAMPLE = min(256, L_SAMPLE // 4)
PEER_HEADS, PEER_NKEYS, PEER_DQ, PEER_TOPK = 8, 128, 128, 16
SLOTS = PEER_HEADS * PEER_TOPK
ALPHA = 2.0 ** 0.25
LN_EPS = 1e-5
ATT_SCALE = HEAD_DIM ** -0.5
IDX_SCALE = (IDX_HEADS * IDX_DIM) ** -0.5
KC = D_MODEL // P
CC = D_CONV // P
MASKED = -1.0e30
TAKEN = -3.0e38
TAKEN_LIMIT = -2.0e38

Z_A, Z_B = 0, D_CONV
Z_Q = Z_B + D_CONV
Z_K = Z_Q + N_HEADS * HEAD_DIM
Z_QI = Z_K + D_KV
Z_KI = Z_QI + IDX_HEADS * IDX_DIM
Z_V = Z_KI + IDX_DIM
Z_WI = Z_V + D_KV
Z_GC = Z_WI + IDX_HEADS
Z_GA = Z_GC + D_MODEL
Z_COLS = Z_GA + D_MODEL
N_ROT = (Z_V - Z_Q) // HEAD_DIM
HEAD_AT = [(2 * (i // 8) + i % 2) * KV_GROUP + i // 2 % KV_GROUP for i in range(N_HEADS)]
BLK = 512
N_BLK = Z_COLS // BLK
BLK_REST = Z_COLS - N_BLK * BLK
RING = 4
CONV_PARAMS = CONV_W + 3
QB = 2 * DEC_SEQ


def build(nc, io):
    with ExitStack() as ctx:
        _build(nc, io, ctx)


def _build(nc, io, ctx):
    class Chain:

        def __init__(self, eng, semaphore):
            self.eng, self.sem, self.n = eng, semaphore, 0

        def restart(self):
            self.until(self.n)
            self.eng.sem_clear(self.sem)
            self.n = 0

        def mark(self, ins):
            ins.then_inc(self.sem, 1)
            self.n += 1
            return self.n

        def until(self, n):
            self.eng.wait_ge(self.sem, n)

        def link(self, ins):
            self.until(self.mark(ins))

    def sb(name, cols, parts=P, dt=F32):
        return ctx.enter_context(nc.sbuf_tensor(name, [parts, cols], dt))

    w_conv_out = sb("w_conv_out_s", CC * D_MODEL)
    w_out = sb("w_out_s", KC * D_MODEL)
    w_query = sb("w_query_s", KC * D_MODEL)
    peer_keys = sb("peer_keys_s", PEER_HEADS * PEER_NKEYS)
    ident = sb("ident_s", P)
    conv_p = sb("conv_p", CC * CONV_PARAMS)
    rope = sb("rope_s", 2 * ROPE_DIM)
    zt = sb("zt", Z_COLS)
    small = sb("small", 944)
    z_stage_b = sb("z_stage_b", BLK)
    keep = sb("keep", N_KV * SEQ + SEQ + N_TILES * D_KV)
    kT = keep[:, 0:2048]
    kiT = keep[:, 2048:2560]
    vrows = keep[:, 2560:3584]
    queries = sb("queries", (N_HEADS + IDX_HEADS) * P)
    qT = queries[:, 0:2048]
    qiT = queries[:, 2048:3072]
    soft_score = sb("soft_score", 5 * SEQ)
    soft = soft_score[:, 0:2048]
    score = soft_score[:, 2048:2560]
    bias = sb("bias", SEQ)
    conv_n = bias
    conv_acc = sb("conv_acc", D_CONV)
    causal = conv_acc
    U_COLS = CC * (P + CONV_W - 1)
    uah = sb("uah", U_COLS + 2 * D_MODEL)
    uT = uah[:, 0:U_COLS]
    actT = uah[:, U_COLS:U_COLS + D_MODEL]
    h_t = uah[:, U_COLS + D_MODEL:]
    eidx = sb("eidx", SLOTS, dt=U32)
    gate = sb("gate", SLOTS)
    late = sb("late", 2 * D_MODEL + RING * P + 6 * SLOTS)
    y_v = late[:, 0:1024]
    h_u = late[:, 1024:2048]
    diag = late[:, 2048:2560]
    gelu_a = late[:, 2560:2688]
    dots = late[:, 2688:2816]
    w_v = late[:, 2816:2944]
    e_v = late[:, 2944:3072].bitcast(U32)
    e_u = late[:, 3072:3200].bitcast(U32)
    g_u = late[:, 3200:3328]
    rings = sb("rings", 2 * RING * D_MODEL)
    rope_tmp = soft[:, 0:2 * N_ROT * ROPE_DIM]

    bank = [ctx.enter_context(nc.psum_tensor(f"bank{i}", [P, BLK], F32)) for i in range(4)]
    acc = ctx.enter_context(nc.psum_tensor("acc", [P, D_MODEL], F32))
    wide = ctx.enter_context(nc.psum_tensor("wide", [P, D_MODEL], F32))
    s_bank = bank[0:2]
    t_bank = bank[2:4]

    zs = nc.dram_tensor("z_rows", (N_TILES + 1, P, Z_COLS), F32, kind="Internal").ap()
    att_s = nc.dram_tensor("att_sample", (DEC_BATCH, P, HEAD_DIM), F32, kind="Internal").ap()
    e_s = nc.dram_tensor("e_sample", (N_SAMPLE, SLOTS), U32, kind="Internal").ap()
    g_s = nc.dram_tensor("g_sample", (N_SAMPLE, SLOTS), F32, kind="Internal").ap()
    h_s = nc.dram_tensor("h_sample", (N_SAMPLE, D_MODEL), F32, kind="Internal").ap()

    xT_a = zt[:, 0:KC * P].rearrange("p (c n) -> p c n", c=KC)
    xT_b = late[:, 0:2 * KC * P].rearrange("p (c n) -> p c n", c=KC)
    xT_c = [y_v.rearrange("p (c n) -> p c n", c=KC),
            diag[:, 0:KC * N_SAMPLE].rearrange("p (c n) -> p c n", c=KC)]
    w_halves = rings[:, RING * D_MODEL:].rearrange("p (r c n) -> p r c n", r=2, c=KC // 2)
    w_ring = rings[:, :].rearrange("p (r c n) -> p r c n", r=2, c=KC)
    z_stage = qT[:, 0:2 * BLK].rearrange("p (s n) -> p s n", s=2)
    wco = w_conv_out[:, :].rearrange("p (c n) -> p c n", c=CC)
    wou = w_out[:, :].rearrange("p (c n) -> p c n", c=KC)
    wqu = w_query[:, :].rearrange("p (c n) -> p c n", c=KC)
    pk = peer_keys[:, :].rearrange("p (h n) -> p h n", h=PEER_HEADS)
    cp = conv_p[:, :].rearrange("p (c n) -> p c n", c=CC)
    kT3 = kT[0:HEAD_DIM, :].rearrange("p (h n) -> p h n", h=N_KV)
    v3 = vrows[:, :].rearrange("p (t n) -> p t n", t=N_TILES)
    qT3 = qT[0:HEAD_DIM, :].rearrange("p (h n) -> p h n", h=N_HEADS)
    qiT3 = qiT[0:IDX_DIM, :].rearrange("p (h n) -> p h n", h=IDX_HEADS)
    sc2 = soft[:, 0:2 * SEQ].rearrange("p (b n) -> p b n", b=2)
    pt2 = soft[:, 2 * SEQ:4 * SEQ].rearrange("p (b n) -> p b n", b=2)
    ln_gb = soft[:, :].rearrange("p (b n) -> p b n", b=2)
    uT3 = uT[:, :].rearrange("p (c n) -> p c n", c=CC)
    ca3 = conv_acc[:, :].rearrange("p (c n) -> p c n", c=CC)
    cy3 = ca3
    aT3 = actT[:, :].rearrange("p (c n) -> p c n", c=KC)
    u_ring = rings[:, 0:RING * D_MODEL].rearrange("p (r n) -> p r n", r=RING)
    v_ring = rings[:, RING * D_MODEL:].rearrange("p (r n) -> p r n", r=RING)
    dg = diag[:, :].rearrange("p (r n) -> p r n", r=RING)

    sk = zt[:, 0:2048].rearrange("p (h s n) -> p h s n", h=PEER_HEADS, s=2)
    cand = zt[:, 2048:4096].rearrange("p (h n) -> p h n", h=PEER_HEADS)
    onehot = qT[:, :].rearrange("p (x n) -> p x n", n=PEER_TOPK)
    qhT = qiT[:, :].rearrange("p (h n) -> p h n", h=PEER_HEADS)
    top_v = actT[:, 0:256].rearrange("p (h s n) -> p h s n", h=PEER_HEADS, s=2)
    top_i = actT[:, 256:512].bitcast(U32).rearrange("p (h s n) -> p h s n", h=PEER_HEADS, s=2)
    top_if = actT[:, 512:768].rearrange("p (h s n) -> p h s n", h=PEER_HEADS, s=2)
    c_val = small[:, 512:640]
    c_idx = small[:, 640:768].bitcast(U32)
    c_row = actT[:, 768:896]
    c_rowu = actT[:, 896:1024].bitcast(U32)
    iota16 = small[:, 768:784]
    f_stats = small[:, 128:140]
    f_mean_var = small[:, 140:142]
    f_rstd = small[:, 142:143]
    quarter = small[:, 784:816]
    zero = small[:, 816:944]
    c_e1 = conv_n[:, 0:128]
    c_e2 = conv_n[:, 128:256]
    row_max = small[:, 0:16]
    neg_max = small[:, 16:32]
    row_sum = small[:, 32:48]
    row_inv = small[:, 48:64]
    stats = small[:, 64:76]
    mean_var = small[:, 76:78]
    rstd = small[:, 78:79]
    top8 = small[:, 80:88]
    wi_s = small[:, 88:96]
    g_max = small[:, 96:104]
    g_sum = small[:, 104:112]
    g_inv = small[:, 112:120]
    logits = small[:, 256:384]
    key_bank = [*t_bank, *s_bank]

    def sem(name):
        return ctx.enter_context(nc.semaphore(name))

    xT_in = sem("xT_in")
    xT_b_in = sem("xT_b_in")
    xT_c_in = sem("xT_c_in")
    w_in = [sem("w_in0"), sem("w_in1")]
    w_in_b = [sem("w_in_b0"), sem("w_in_b1")]
    w_in_c = [sem("w_in_c0"), sem("w_in_c1")]
    consts_in = sem("consts_in")
    weights_in = sem("weights_in")
    projected = sem("projected")
    z_copied = sem("z_copied")
    z_stored = [sem(f"z_stored{k}") for k in range(2)]
    projected_b = sem("projected_b")
    z_copied_b = sem("z_copied_b")
    z_stored_b = sem("z_stored_b")
    projected_c = sem("projected_c")
    z_copied_c = sem("z_copied_c")
    z_stored_c = sem("z_stored_c")
    half_used = sem("half_used")
    z_loaded = sem("z_loaded")
    sig_b = sem("sig_b")
    u_ready = sem("u_ready")
    roped = sem("roped")
    rows_out = sem("rows_out")
    v_kept = sem("v_kept")
    transposed = sem("transposed")
    t_copied = sem("t_copied")
    idx_mm = sem("idx_mm")
    idx_relu = sem("idx_relu")
    idx_used = sem("idx_used")
    qk_mm = sem("qk_mm")
    maxed = sem("maxed")
    exped = sem("exped")
    p_trans = sem("p_trans")
    p_copied = sem("p_copied")
    pv_mm = sem("pv_mm")
    att_ready = sem("att_ready")
    conv_done = sem("conv_done")
    conv_t = sem("conv_t")
    conv_normed = sem("conv_normed")
    conv_t2 = sem("conv_t2")
    conv_act = sem("conv_act")
    conv_mm = sem("conv_mm")
    gates_ready = sem("gates_ready")
    merged = sem("merged")
    m_trans = sem("m_trans")
    m_copied = sem("m_copied")
    out_mm = sem("out_mm")
    x_in = sem("x_in")
    h_ready = sem("h_ready")
    ln2_in = sem("ln2_in")
    h_trans = sem("h_trans")
    h_copied = sem("h_copied")
    pq_mm = sem("pq_mm")
    pq_copied = sem("pq_copied")
    key_mm = sem("key_mm")
    key_copied = sem("key_copied")
    logits_ready = sem("logits_ready")
    exp_ready = sem("exp_ready")
    var_ready = sem("var_ready")
    std_ready = sem("std_ready")
    routed = sem("routed")
    eu_ready = sem("eu_ready")
    gu_ready = sem("gu_ready")
    ev_ready = sem("ev_ready")
    hu_read = sem("hu_read")
    hu_ready = sem("hu_ready")
    u_in = [sem(f"u_in{k}") for k in range(RING)]
    v_in = [sem(f"v_in{k}") for k in range(RING)]
    dotted = sem("dotted")
    gelued = sem("gelued")
    weighted = sem("weighted")
    diag_ready = sem("diag_ready")
    summed = sem("summed")
    added = sem("added")
    acc_taken = sem("acc_taken")
    var2_ready = sem("var2_ready")
    std2_ready = sem("std2_ready")
    y_ready = sem("y_ready")
    y_stored = sem("y_stored")
    dve_chain = sem("dve_chain")
    act_chain = sem("act_chain")
    passed = sem("passed")
    scratch = sem("scratch")
    scratch_in = sem("scratch_in")
    table_in = sem("table_in")
    page_in = sem("page_in")
    kidx_in = [sem("kidx_in0"), sem("kidx_in1")]
    v_pages_in = [sem("v_pages_in0"), sem("v_pages_in1")]
    vnew_in = sem("vnew_in")
    w_query_in = sem("w_query_in")
    k_in = [sem("k_in0"), sem("k_in1")]
    s_idx_mm = sem("s_idx_mm")
    s_idx_relu = sem("s_idx_relu")
    s_idx_sum = sem("s_idx_sum")
    s_wsel = sem("s_wsel")
    s_summed_out = sem("s_summed_out")
    s_bias = sem("s_bias")
    s_qbd = sem("s_qbd")
    s_qk = sem("s_qk")
    s_max = sem("s_max")
    s_exp = sem("s_exp")
    s_pt = sem("s_pt")
    s_ptc = sem("s_ptc")
    s_pv = sem("s_pv")
    s_o = sem("s_o")
    s_rows = sem("s_rows")
    s_new = sem("s_new")
    s_zero = sem("s_zero")


    K_COLS = L_SAMPLE
    kv_buf = w_query[:, :].rearrange("p (i n) -> p i n", i=2)
    smp_k = [kv_buf[:, i, 0:2 * PAST_LEN].rearrange("p (j n) -> p j n", j=2) for i in range(2)]
    smp_v = [kv_buf[:, i, 2 * PAST_LEN:].rearrange("p (t n) -> p t n", t=N_PAGES) for i in range(2)]
    smp_vnew = zt[0:DEC_SEQ, 0:DEC_BATCH * D_KV].rearrange("p (b n) -> p b n", b=DEC_BATCH)
    smp_kinew = keep[0:IDX_DIM, 2304:2336]
    smp_knew = keep[:, 2336:2400].rearrange("p (j n) -> p j n", j=2)
    smp_e = vrows[0:N_SAMPLE, :].rearrange("p (b n) -> p b n", b=DEC_BATCH)
    smp_p = soft_score[:, 0:K_COLS]
    smp_ki = [soft_score[0:IDX_DIM, K_COLS:K_COLS + PAST_LEN], keep[0:IDX_DIM, 0:PAST_LEN]]
    smp_wb = [soft_score[0:N_SAMPLE, 2056 + 32 * i:2088 + 32 * i] for i in range(2)]
    smp_qi = [soft_score[0:IDX_DIM, 2120 + 32 * i:2152 + 32 * i].rearrange("p (h n) -> p h n", h=IDX_HEADS)
              for i in range(2)]
    smp_qbd = soft_score[:, 2184:2312].rearrange("p (j n) -> p j n", j=2)
    smp_eb = soft_score[0:N_SAMPLE, 2312:2440]
    smp_o = soft_score[:, 2440:2504]
    smp_score = uah[0:N_SAMPLE, 0:K_COLS]
    smp_relu = uah[0:N_SAMPLE, K_COLS:2 * K_COLS]
    smp_uTf = queries[:, 0:CC * DEC_BATCH * 34]
    smp_uT = smp_uTf.rearrange("p (c b n) -> p c b n", c=CC, b=DEC_BATCH)
    smp_qiT = queries[0:IDX_DIM, 1088:1344]
    smp_pt = queries[:, 1344:2496].rearrange("p (t n) -> p t n", t=N_PAGES + 1)
    smp_qall = queries[:, 2496:2816].rearrange("p (j h n) -> p j h n", j=2, h=KV_GROUP)
    smp_choose = queries[0:N_SAMPLE, 2816:3072]
    smp_sel = smp_choose.rearrange("p (b n) -> p b n", b=DEC_BATCH)
    smp_causal = small[0:N_SAMPLE, 168:168 + DEC_SEQ]
    smp_wi = small[0:N_SAMPLE, 160:168]
    smp_stat = small[:, 176:190]
    smp_acc3 = conv_acc[:, 0:CC * N_SAMPLE].rearrange("p (c b n) -> p c b n", c=CC, b=DEC_BATCH)
    smp_acc = conv_acc[:, 0:CC * N_SAMPLE].rearrange("p (c n) -> p c n", c=CC)
    page_s = small[0:1, 192:192 + DEC_BATCH * N_PAGES].bitcast(I32)
    def wait_apart(eng, semaphore, value):
        eng.wait_ge(semaphore, value)
        eng.sem_inc(passed, 1)

    S_T = N_TILES
    block = ctx.enter_context(nc.Block())
    GROUPS = 9
    LAG = 6
    N_STEPS = SLOTS + LAG
    N_GROUPS_B = 2 * (N_BLK + 1)
    Q_SLOTS = SLOTS // 4
    PROJ_EARLY = 0.6
    AT_IDX, AT_TOPK, AT_ATT, AT_TAIL, AT_PEER = 0.05, 0.09, 0.20, 0.48, 0.71
    HEAD_STEP = (AT_TAIL - AT_ATT) / N_HEADS
    AT_S_SUM, AT_S_TOPK, AT_S_ATT, AT_S_TAIL, AT_S_END = 0.05, 0.27, 0.58, 1.10, 1.9
    S_IDX_STEP = (AT_S_TOPK - AT_S_SUM) / DEC_BATCH
    S_ATT_STEP = (AT_S_TAIL - AT_S_ATT) / (DEC_BATCH + 0.2)

    LAST = N_TILES - 1

    def is_tile(v, *tiles):
        return isinstance(v, int) and v in tiles

    DVE_FROM = int(AT_S_ATT * N_STEPS) - LAG
    V_SLOTS = {LAST - 1: SLOTS, LAST: SLOTS, S_T: Q_SLOTS}
    dve_slots = {LAST - 1: [s for s in range(DVE_FROM, SLOTS) if s % 2], LAST: list(range(1, SLOTS, 2)), S_T: []}
    pe_slots = {v: [s for s in range(n) if s not in dve_slots[v]] for v, n in V_SLOTS.items()}

    def on_pe(v, s):
        return not is_tile(v, *V_SLOTS) or s in pe_slots[v]

    def number(v, s):
        return (pe_slots[v] if on_pe(v, s) else dve_slots[v]).index(s) if is_tile(v, *V_SLOTS) else s

    def summed_before(v):
        if is_tile(v, LAST, S_T):
            return (LAST - 1) * SLOTS + sum(len(pe_slots[k]) for k in range(LAST - 1, v))
        return v * SLOTS

    def added_before(v):
        return sum(len(dve_slots[k]) for k in range(LAST - 1, v))

    PER_TILE = 16 * SLOTS // RING

    def home(v, s):
        if not is_tile(v, LAST, S_T):
            return v_ring, s % RING, v_in, v * PER_TILE + (s // RING * 16 + 16)
        place = s // 2 % RING
        landed = s // 2 // RING * 16 + 16 + (PER_TILE // 2 if v == S_T else 0)
        if s % 2:
            return u_ring, place, u_in, N_TILES * PER_TILE + landed + (Q_SLOTS * 16 // RING if v == S_T else 0)
        return v_ring, place, v_in, LAST * PER_TILE + landed

    def conv_at(x, n):
        return x if n == P else AT_S_TOPK + 0.04 + (x - AT_TAIL) * 2.5

    def tail_at(x, n):
        return x if n == P else AT_S_TAIL + (x - 0.54) * (AT_S_END - AT_S_TAIL) / (1.0 - 0.54)

    def group_at(g, last=1.0):
        x = g / N_GROUPS_B
        return x / PROJ_EARLY * AT_TAIL if x < PROJ_EARLY else \
            AT_PEER + (x - PROJ_EARLY) / (1 - PROJ_EARLY) * (last - AT_PEER)

    half_at = {int(group_at(k - 1, 0.95) * N_STEPS) + 2: k for k in range(2, 2 * N_BLK + 2)}

    class Strand:

        def __init__(self, pieces):
            self.pieces = pieces
            self.at = next(pieces, None)

        def step(self):
            self.at = next(self.pieces, None)

    def weave(front, slots, upto=None):
        while slots.at is not None or (front.at is not None and (upto is None or front.at < upto)):
            if slots.at is None or (front.at is not None and front.at < slots.at and (upto is None or front.at < upto)):
                front.step()
            else:
                slots.step()

    def nothing():
        return Strand(iter(()))

    @block.sync
    def _(sp):
        sp.dma_start(page_s[:, :], io["page_table"]).then_inc(table_in, 16)
        sp.dma_start(xT_a, io["xT_a"]).then_inc(xT_in, 16)
        for r in range(2):
            sp.dma_start(w_ring[:, r], io["w_in"][r]).then_inc(w_in[r], 16)
        with sp.Fori(1, N_BLK // 2) as i:
            for r in range(2):
                sp.wait_ge(projected, i * 2 + (r - 1))
                sp.dma_start(w_ring[:, r], io["w_in"][i * 2 + r]).then_inc(w_in[r], 16)
        sp.wait_ge(projected, N_BLK - 1)
        sp.dma_start(w_ring[:, 0, :, 0:BLK_REST], io["w_in_rest"]).then_inc(w_in[0], 16)
        sp.dma_start(xT_b, io["xT_b"]).then_inc(xT_b_in, 16)
        for k in range(2):
            sp.wait_ge(z_stored[k], 16 * (N_BLK // 2 + 1) + 16 * (k < 1))

        def tile_loads(t, n):
            sp.wait_ge(routed, t + 1)
            sp.dma_start(zt[0:n, :], zs[t, 0:n, :]).then_inc(z_loaded, 16)
            sp.dma_start(rope[0:n, :], io["rope"][t, 0:n, :]).then_inc(z_loaded, 16)

        def norm_loads(t, n, x_rows):
            sp.wait_ge(hu_ready, t + 1)
            sp.dma_start(h_t[0:n, :], x_rows).then_inc(x_in, 16)
            sp.dma_start(ln_gb[0:n], io["ln1"].partition_broadcast(n)).then_inc(x_in, 16)

        def front(t):
            tile_loads(t, P)
            sp.dma_start(causal[:, :], io["causal"][t]).then_inc(z_loaded, 16)
            sp.wait_ge(u_ready, t + 1)
            sp.dma_start(io["conv_prompt"], zt[P - (CONV_W - 1):P, Z_A:Z_A + D_CONV]).then_inc(rows_out, 16)
            sp.wait_ge(roped, t + 1)
            sp.dma_start(io["k_prompt"][t], zt[:, Z_K:Z_K + D_KV]).then_inc(rows_out, 16)
            sp.dma_start(io["v_prompt"][t], zt[:, Z_V:Z_V + D_KV]).then_inc(rows_out, 16)
            sp.dma_start(io["kidx_prompt"][t], zt[:, Z_KI:Z_KI + IDX_DIM]).then_inc(rows_out, 16)
            sp.wait_ge(pv_mm, t * N_HEADS + N_HEADS)
            norm_loads(t, P, io["x_rows"][t])

        def finish(t, n, total, out):
            sp.wait_ge(summed, total)
            if is_tile(t, LAST - 1):
                sp.wait_ge(added, added_before(LAST) + 1)
            sp.dma_start(v_ring[0:n, 0:2, :], io["ln2"].partition_broadcast(n)).then_inc(ln2_in, 16)
            sp.wait_ge(y_ready, t + 1)
            sp.dma_start(out, v_ring[0:n, 2, :]).then_inc(y_stored, 16)

        def page(b, j):
            at = b * N_PAGES + j
            return sp.value_load(page_s[0:1, at:at + 1], min_val=0, max_val=N_POOL - 1)

        def index_pages(b):
            pages = [page(b, j) for j in range(N_PAGES)]
            if b >= 2:
                sp.wait_ge(s_idx_mm, b - 1)
            for j in range(N_PAGES):
                sp.dma_start(smp_ki[b % 2][:, j * PAGE:(j + 1) * PAGE],
                             io["kidx_T"][pages[j]]).then_inc(kidx_in[b % 2], 16)

        def front_sample():
            n = N_SAMPLE
            yield 0.0
            tile_loads(S_T, n)
            sp.dma_start(smp_causal, io["causal_sample"]).then_inc(z_loaded, 16)
            sp.dma_start(smp_uTf, io["state_T"]).then_inc(page_in, 16)
            sp.dma_start(vrows[0:n, :], io["spread"]).then_inc(page_in, 16)
            sp.dma_start(smp_choose, io["choose"]).then_inc(page_in, 16)
            for h in range(IDX_HEADS):
                sp.dma_start(smp_wi[h * DEC_SEQ:(h + 1) * DEC_SEQ, :],
                             zs[S_T, 0:n, Z_WI + h].rearrange("(b q) -> q b", q=DEC_SEQ),
                             allow_slow_non_contiguous=True).then_inc(page_in, 16)
            sp.wait_ge(table_in, 16)
            for b in range(2):
                index_pages(b)
            sp.wait_ge(u_ready, S_T + 1)
            sp.dma_start(io["conv_sample"][:, CONV_W - 1 - DEC_SEQ:, :],
                         zt[0:n, Z_A:Z_A + D_CONV]).then_inc(rows_out, 16)
            sp.dma_start(io["conv_sample"][:, 0:CONV_W - 1 - DEC_SEQ, :],
                         io["state_conv"][:, DEC_SEQ:, :]).then_inc(rows_out, 16)
            sp.wait_ge(roped, S_T + 1)
            sp.dma_start(io["k_sample"], zt[0:n, Z_K:Z_K + D_KV]).then_inc(rows_out, 16)
            sp.dma_start(io["v_sample"], zt[0:n, Z_V:Z_V + D_KV]).then_inc(rows_out, 16)
            sp.dma_start(io["kidx_sample"], zt[0:n, Z_KI:Z_KI + IDX_DIM]).then_inc(rows_out, 16)
            for b in range(2, DEC_BATCH):
                yield AT_S_SUM + (b - 1) * S_IDX_STEP
                index_pages(b)
            yield AT_S_TOPK + 0.01
            sp.wait_ge(rows_out, 64 * N_TILES + 80)
            sp.wait_ge(t_copied, N_TILES * GROUPS + 5)
            sp.dma_start(smp_vnew, zs[S_T, 0:n, Z_V:Z_V + D_KV].rearrange("(b q) n -> q b n",
                                                                          q=DEC_SEQ)).then_inc(vnew_in, 16)
            for b in range(DEC_BATCH):
                if b >= 2:
                    yield AT_S_ATT + (b - 1.2) * S_ATT_STEP
                pages = [page(b, j) for j in range(N_PAGES)]
                if b >= 2:
                    sp.wait_ge(s_qk, b - 1)
                for j in range(N_PAGES):
                    sp.dma_start(smp_k[b % 2][:, :, j * PAGE:(j + 1) * PAGE],
                                 io["cache_kT"][pages[j]].rearrange("p (j n) -> p j n", j=2)).then_inc(k_in[b % 2], 16)
                if b >= 2:
                    yield AT_S_ATT + (b - 1.0) * S_ATT_STEP
                    sp.wait_ge(s_pv, b)
                for j in range(N_PAGES):
                    sp.dma_start(smp_v[b % 2][:, j, :], io["cache_v"][pages[j]]).then_inc(v_pages_in[b % 2], 16)
                if b >= 2:
                    sp.wait_ge(s_o, b)
                    sp.dma_start(att_s[b - 2], smp_o).then_inc(s_rows, 16)
            yield AT_S_ATT + (DEC_BATCH - 1 + 0.2) * S_ATT_STEP
            sp.wait_ge(s_o, DEC_BATCH)
            sp.dma_start(att_s[DEC_BATCH - 2], smp_o).then_inc(s_rows, 16)
            yield AT_S_TAIL - 0.01
            sp.wait_ge(s_pv, DEC_BATCH + 1)
            sp.dma_start(w_query[:, :], io["w_query"]).then_inc(w_query_in, 16)
            sp.wait_ge(s_o, DEC_BATCH + 1)
            sp.dma_start(att_s[DEC_BATCH - 1], smp_o).then_inc(s_rows, 16)
            sp.wait_ge(s_rows, 16 * DEC_BATCH + 16)
            for b in range(DEC_BATCH):
                rows = att_s[b].rearrange("(h q) d -> q h d", q=QB)[0:DEC_SEQ]
                dst = zt[b * DEC_SEQ:(b + 1) * DEC_SEQ, Z_Q:Z_Q + D_MODEL].rearrange("q (h d) -> q h d", h=N_HEADS)
                sp.dma_start(dst, rows).then_inc(scratch_in, 16)
            norm_loads(S_T, n, io["x_rows"][S_T, 0:n, :])

        front(0)
        sp.wait_ge(projected_b, N_GROUPS_B)
        for j in range(2):
            sp.dma_start(xT_c[j], io[f"xT_c{j}"]).then_inc(xT_c_in, 16)
        sp.wait_ge(z_stored_b, 16 * N_GROUPS_B)
        front(1)
        sp.wait_ge(z_stored_c, 16 * N_GROUPS_B)
        with sp.Fori(1, N_TILES - 1) as t:
            front(t + 1)
            finish(t - 1, P, summed_before(t) + RING, io["y_prompt"][t - 1])
        sample = Strand(front_sample())
        weave(sample, nothing(), 1.0)
        finish(N_TILES - 2, P, summed_before(N_TILES - 1) + RING, io["y_prompt"][N_TILES - 2])
        weave(sample, nothing())
        n = N_SAMPLE
        sp.wait_ge(routed, S_T + 2)
        sp.dma_start(e_s, eidx[0:n, :]).then_inc(scratch, 16)
        sp.dma_start(g_s, gate[0:n, :]).then_inc(scratch, 16)
        sp.dma_start(h_s, h_t[0:n, :]).then_inc(scratch, 16)
        sp.wait_ge(scratch, 48)
        sp.wait_ge(weighted, N_TILES)
        sp.wait_ge(hu_read, N_TILES)
        for k in range(4):
            rows, cols = slice(n * k, n * (k + 1)), slice(Q_SLOTS * k, Q_SLOTS * (k + 1))
            sp.dma_start(e_u[rows, 0:Q_SLOTS], e_s[:, cols]).then_inc(scratch_in, 16)
            sp.dma_start(g_u[rows, 0:Q_SLOTS], g_s[:, cols]).then_inc(scratch_in, 16)
            sp.dma_start(h_u[rows, :], h_s).then_inc(scratch_in, 16)
        finish(N_TILES - 1, P, summed_before(S_T) + RING, io["y_prompt"][N_TILES - 1])
        finish(S_T, n, summed_before(S_T) + Q_SLOTS + RING, io["y_sample"])
        sp.wait_ge(y_stored, 16 * (N_TILES + 2))
        sp.wait_ge(rows_out, 64 * N_TILES + 80)

    @block.gpsimd
    def _(pool):
        for dst in (uT, kT, kiT, vrows):
            nc.gpsimd.memset(dst, 0.0).then_inc(s_zero, 1)
        nc.gpsimd.memset(zero, 0.0).then_inc(s_zero, 1)
        for s_ in (eu_ready, gu_ready):
            pool.sem_inc(s_, 1)
        for dst, src in ((ident, "ident"), (conv_p, "conv_params")):
            pool.dma_start(dst[:, :], io[src]).then_inc(consts_in, 16)
        pool.dma_start(iota16, io["iota16"]).then_inc(consts_in, 16)
        pool.dma_start(quarter, io["quarter"]).then_inc(consts_in, 16)
        pool.wait_ge(s_zero, 5)

        def keep_values(t):
            pool.wait_ge(z_loaded, 48 * t + 48)
            nc.gpsimd.tensor_copy(v3[:, t, :], zt[:, Z_V:Z_V + D_KV]).then_inc(v_kept, 1)

        def hand_over(u, v):
            if v is not None:
                pool.wait_ge(dotted, v * SLOTS + SLOTS + RING)
                wait_apart(pool, summed, summed_before(v) + RING)
                if is_tile(v, LAST):
                    pool.wait_ge(added, added_before(v) + 1)
                nc.gpsimd.tensor_copy(e_v, e_u).then_inc(ev_ready, 1)
                wait_apart(pool, ev_ready, v + 1)
            if u is not None:
                wait_apart(pool, routed, u + 2)
                nc.gpsimd.tensor_copy(e_u, eidx[:, :]).then_inc(eu_ready, 1)
                if v is not None:
                    wait_apart(pool, weighted, v + 1)
                nc.gpsimd.tensor_copy(g_u, gate[:, :]).then_inc(gu_ready, 1)
                wait_apart(pool, eu_ready, u + 2)

        def fetch(ring, place, table, numbers, s, done):
            offs = bass.IndirectOffsetOnAxis(ap=numbers[:, s:s + 1], axis=0)
            nc.gpsimd.indirect_dma_start(ring[:, place, :], None, table, offs).then_inc(done[place], 16)

        def fetch_u(u, s):
            if s == 0 and is_tile(u, S_T):
                pool.wait_ge(added, added_before(S_T) + 1)
            wait_apart(pool, dotted, u * SLOTS + s + 1)
            fetch(u_ring, s % RING, io["peer_u"], e_u, s, u_in)

        def fetch_v(v, s):
            ring, place, done, _ = home(v, s)
            if s == 0:
                wait_apart(pool, y_stored, v * 16 + 16)
            else:
                back = s - (2 * RING if is_tile(v, LAST, S_T) else RING)
                if back >= 0 and on_pe(v, back):
                    wait_apart(pool, summed, summed_before(v) + (number(v, back) + 1 + RING))
                elif back >= 0:
                    pool.wait_ge(added, added_before(v) + number(v, back) + 2)
            fetch(ring, place, io["peer_v"], e_v, s, done)

        keep_values(0)
        pool.wait_ge(projected, N_BLK + 1)
        later_weights = {1: (w_conv_out, "w_conv_out"), 2: (w_out, "w_out"), 4: (w_query, "w_query"),
                         5: (peer_keys, "peer_keys")}
        for i in range(N_BLK + 1):
            if i >= 2:
                pool.wait_ge(projected_b, 2 * (i - 1))
            dst, src = (w_ring[:, i % 2], io["w_in"][i]) if i < N_BLK else (w_ring[:, i % 2, :, 0:BLK_REST],
                                                                            io["w_in_rest"])
            pool.dma_start(dst, src).then_inc(w_in_b[i % 2], 16)
            if i in later_weights:
                dst, src = later_weights[i]
                pool.dma_start(dst[:, :], io[src]).then_inc(weights_in, 16)
        pool.wait_ge(projected_b, N_GROUPS_B)

        def fetch_half(k):
            i, half = k // 2, k % 2
            if i >= 1:
                if half == 0:
                    pool.wait_ge(half_used, i)
                else:
                    pool.wait_ge(projected_c, 2 * i)
            rows = slice(KC // 2 * half, KC // 2 * (half + 1))
            if i < N_BLK:
                pool.dma_start(w_halves[:, half], io["w_in"][i][:, rows, :]).then_inc(w_in_c[half], 16)
            else:
                pool.dma_start(w_halves[:, half, :, 0:BLK_REST], io["w_in_rest"][:, rows, :]).then_inc(w_in_c[half], 16)

        fetch_half(0)
        fetch_half(1)
        hand_over(0, None)
        for s in range(SLOTS):
            if s in half_at:
                fetch_half(half_at[s])
            fetch_u(0, s)
            if s == 6:
                keep_values(1)
        with pool.Fori(1, N_TILES - 1) as t:
            hand_over(t, t - 1)
            for s in range(N_STEPS):
                if s < SLOTS:
                    fetch_u(t, s)
                if s >= LAG:
                    fetch_v(t - 1, s - LAG)
                if s == 6:
                    keep_values(t + 1)
        hand_over(N_TILES - 1, N_TILES - 2)
        for s in range(N_STEPS):
            if s < SLOTS:
                fetch_u(N_TILES - 1, s)
            if s >= LAG:
                fetch_v(N_TILES - 2, s - LAG)
            if s == 2:
                pool.wait_ge(routed, S_T + 1)
                nc.gpsimd.memset(smp_qall, 0.0).then_inc(s_zero, 1)
                nc.gpsimd.memset(smp_qbd, 0.0).then_inc(s_zero, 1)
        hand_over(None, N_TILES - 1)
        for s in range(SLOTS):
            fetch_v(N_TILES - 1, s)
        pool.wait_ge(scratch_in, 16 * 20)
        for s in range(Q_SLOTS):
            fetch_u(S_T, s)
        pool.wait_ge(summed, summed_before(S_T) + RING)
        nc.gpsimd.tensor_copy(e_v, e_u).then_inc(ev_ready, 1)
        pool.wait_ge(ev_ready, S_T + 1)
        for s in range(Q_SLOTS):
            if s % 2 and s < 2 * RING:
                pool.wait_ge(dotted, S_T * SLOTS + Q_SLOTS - RING + s // 2 + 1 + RING)
            fetch_v(S_T, s)

    @block.scalar
    def _(act):
        chain = Chain(act, act_chain)
        act.sem_inc(z_copied, 2)
        for k in range(2):
            act.sem_inc(z_stored[k], 16)
        act.sem_inc(y_stored, 16)
        act.sem_inc(hu_ready, 1)

        def store_block(i, r, width):
            act.wait_ge(projected, i * 2 + (r + 1))
            act.wait_ge(z_stored[r], i * 16 + 16)
            nc.scalar.copy(z_stage[:, r, 0:width], bank[r][:, 0:width]).then_inc(z_copied, 1)
            act.wait_ge(z_copied, i * 2 + (r + 3))
            act.dma_start(zs[0, :, bass.ds(i * (2 * BLK) + r * BLK, width)],
                          z_stage[:, r, 0:width]).then_inc(z_stored[r], 16)

        with act.Fori(0, N_BLK // 2) as i:
            store_block(i, 0, BLK)
            store_block(i, 1, BLK)
        store_block(N_BLK // 2, 0, BLK_REST)

        def store_blocks(first, at, ready, copied, stored):
            for g in range(N_GROUPS_B):
                yield at(g)
                i, t = g // 2, first + g % 2
                n = P if t < S_T else N_SAMPLE
                width = BLK if i < N_BLK else BLK_REST
                act.wait_ge(ready, g + 1)
                if g:
                    act.wait_ge(stored, 16 * g)
                nc.scalar.copy(z_stage_b[0:n, 0:width], acc[0:n, g % 2 * BLK:g % 2 * BLK + width]).then_inc(copied, 1)
                act.wait_ge(copied, g + 1)
                act.dma_start(zs[t, 0:n, i * BLK:i * BLK + width], z_stage_b[0:n, 0:width]).then_inc(stored, 16)

        def gates(t, n):
            act.wait_ge(z_loaded, 48 * t + 48)
            nc.scalar.activation(zt[0:n, Z_B:Z_B + D_CONV], zt[0:n, Z_B:Z_B + D_CONV], ACT.Sigmoid).then_inc(sig_b, 1)
            nc.scalar.activation(zt[0:n, Z_GC:], zt[0:n, Z_GC:], ACT.Sigmoid).then_inc(gates_ready, 1)

        def copy_group(g, dst, src):
            act.wait_ge(transposed, g + 1)
            nc.scalar.copy(dst, src).then_inc(t_copied, 1)

        def deviation(number, n):
            act.wait_ge(var_ready, number + 1)
            nc.scalar.activation(rstd[0:n, :], mean_var[0:n, 1:2], ACT.Sqrt).then_inc(std_ready, 1)

        def conv(t, n):
            yield conv_at(0.487, n)
            deviation(2 * t, n)
            yield conv_at(0.50, n)
            act.wait_ge(conv_t2, t + 1)
            for c in range(CC):
                last = nc.scalar.activation(cy3[:, c, 0:n], t_bank[1][:, c * P:c * P + n], ACT.Silu,
                                            scale=cp[:, c, CONV_W + 1:CONV_W + 2],
                                            bias=cp[:, c, CONV_W + 2:CONV_W + 3])
            last.then_inc(conv_act, 1)

        def tail(t, n):
            quarters = lambda x: x[:, :].rearrange("p (c n) -> p c n", c=4)[:, :, 0:n]
            for r in range(2):
                yield tail_at(0.552 + 0.003 * r, n)
                act.wait_ge(m_trans, 2 * t + r + 1)
                nc.scalar.copy(aT3[:, 4 * r:4 * r + 4, 0:n], quarters(t_bank[r])).then_inc(m_copied, 1)
            yield tail_at(0.622, n)
            act.wait_ge(out_mm, t + 1)
            deviation(2 * t + 1, n)
            for r in range(2):
                yield tail_at(0.642 + 0.003 * r, n)
                act.wait_ge(h_trans, 2 * t + r + 1)
                nc.scalar.copy(aT3[:, 4 * r:4 * r + 4, 0:n], quarters(t_bank[r])).then_inc(h_copied, 1)
            for r in range(2):
                yield tail_at(0.675 + 0.023 * r, n)
                act.wait_ge(pq_mm, 2 * t + r + 1)
                nc.scalar.copy(qhT[:, 4 * r:4 * r + 4, 0:n], quarters(s_bank[r])).then_inc(pq_copied, 1)
            act.wait_ge(rows_out, 64 * t + 64 if n == P else 64 * t + 80)
            for j in range(4):
                yield tail_at(0.705, n)
                if j == 0:
                    act.wait_ge(key_mm, 4 * t + 4)
                nc.scalar.copy(sk[0:n, 4 * (j // 2):4 * (j // 2) + 4, j % 2, :],
                               key_bank[j][0:n, :].rearrange("p (h n) -> p h n", h=4)).then_inc(key_copied, 1)
            yield tail_at(0.93, n)
            act.wait_ge(logits_ready, t + 1)
            act.wait_ge(gu_ready, t + 1)
            nc.scalar.activation(gate[0:n, :], logits[0:n, :], ACT.Exp).then_inc(exp_ready, 1)

        def front(t):
            yield 0.0
            gates(t, P)
            here = bass.ds(t * P, P)
            t_view = [b[:, :].rearrange("p (c n) -> p c n", c=4) for b in t_bank]
            yield 0.025
            copy_group(t * GROUPS, kT3[:, :, here], t_view[0][0:HEAD_DIM])
            copy_group(t * GROUPS + 1, kiT[0:IDX_DIM, here], t_bank[1][0:IDX_DIM, 0:P])
            for g in range(2):
                yield 0.03
                copy_group(t * GROUPS + 2 + g, qiT3[:, 4 * g:4 * g + 4, :], t_view[g % 2][0:IDX_DIM])
            for g in range(4):
                yield 0.035 + 0.002 * g
                copy_group(t * GROUPS + 4 + g, qT3[:, 4 * g:4 * g + 4, :], t_view[g % 2][0:HEAD_DIM])
            chain.link(nc.scalar.copy(uT3[:, :, 0:CONV_W - 1], uT3[:, :, P:P + CONV_W - 1]))
            chain.restart()
            copy_group(t * GROUPS + 8, uT3[:, :, CONV_W - 1:], t_view[0])
            for h in range(IDX_HEADS):
                yield AT_IDX + 0.005 * h + 0.001
                act.wait_ge(idx_mm, t * IDX_HEADS + h + 1)
                if h >= 2:
                    act.wait_ge(idx_used, t * IDX_HEADS + h - 1)
                nc.scalar.activation(sc2[:, h % 2, :], s_bank[h % 2][:, :], ACT.Relu).then_inc(idx_relu, 1)

            def exp(h):
                act.wait_ge(maxed, t * N_HEADS + h + 1)
                nc.scalar.activation(sc2[:, h % 2, :], sc2[:, h % 2, :], ACT.Exp, bias=neg_max[:, h:h + 1],
                                     scale=ATT_SCALE, accum_out=row_sum[:, HEAD_AT[h]:HEAD_AT[h] + 1]).then_inc(exped, 1)

            yield AT_ATT
            exp(0)
            for h in range(N_HEADS):
                if h + 1 < N_HEADS:
                    yield AT_ATT + (h + 1) * HEAD_STEP
                    exp(h + 1)
                yield AT_ATT + (h + 1.05) * HEAD_STEP
                act.wait_ge(p_trans, t * N_HEADS + h + 1)
                if h >= 2:
                    act.wait_ge(pv_mm, t * N_HEADS + h - 1)
                nc.scalar.copy(pt2[:, h % 2, :], t_bank[h % 2][:, :]).then_inc(p_copied, 1)
            yield from conv(t, P)
            yield from tail(t, P)

        def front_sample():
            n = N_SAMPLE
            yield 0.0
            gates(S_T, n)
            act.wait_ge(page_in, 16 * 11)
            base = N_TILES * GROUPS
            yield 0.025
            copy_group(base, smp_knew, t_bank[0][:, 0:2 * n].rearrange("p (j n) -> p j n", j=2))
            copy_group(base + 1, smp_kinew, t_bank[1][0:IDX_DIM, 0:n])
            yield 0.03
            copy_group(base + 2, smp_qiT, t_bank[0][0:IDX_DIM, 0:IDX_HEADS * n])
            act.wait_ge(s_zero, 7)
            copy_group(base + 3, smp_qall[:, :, :, 0:n],
                       t_bank[1][:, 0:8 * n].rearrange("p (j h n) -> p j h n", j=2, h=KV_GROUP))
            act.wait_ge(transposed, base + 5)
            for c in range(CC):
                last = nc.scalar.copy(smp_uT[:, c, :, CONV_W - 1:],
                                      t_bank[0][:, c * n:(c + 1) * n].rearrange("p (b q) -> p b q", b=DEC_BATCH))
            last.then_inc(t_copied, 1)
            act.wait_ge(t_copied, base + 5)
            act.sem_inc(s_idx_sum, 2)
            act.sem_inc(s_pv, 1)
            act.sem_inc(s_idx_relu, 1)
            act.sem_inc(s_o, 1)
            act.sem_inc(s_rows, 16)
            qi_all = smp_qiT.rearrange("p (h n) -> p h n", h=IDX_HEADS)
            for b in range(DEC_BATCH):
                new = slice(b * DEC_SEQ, (b + 1) * DEC_SEQ)
                yield AT_S_SUM + b * S_IDX_STEP
                if b >= 2:
                    act.wait_ge(s_idx_mm, b - 1)
                nc.scalar.copy(smp_qi[b % 2], qi_all[:, :, new]).then_inc(s_new, 1)
                yield AT_S_SUM + (b + 0.3) * S_IDX_STEP
                act.wait_ge(s_idx_mm, b + 1)
                act.wait_ge(s_idx_sum, b + 2)
                nc.scalar.activation(smp_relu[:, 0:BLK], s_bank[0][0:n, :], ACT.Relu)
                nc.scalar.activation(smp_relu[:, BLK:2 * BLK], s_bank[1][0:n, :], ACT.Relu)
                nc.scalar.activation(smp_relu[:, 2 * BLK:], t_bank[0][0:n, 0:DEC_SEQ],
                                     ACT.Relu).then_inc(s_idx_relu, 1)

            yield from conv(S_T, n)

            def queries_of(b):
                if b:
                    act.wait_ge(s_qk, b)
                for half in range(2):
                    rows = slice(HEAD_DIM * half, HEAD_DIM * (half + 1))
                    nc.scalar.copy(smp_qbd[rows, :, 32 * half:32 * half + 32].rearrange("p j (h q) -> p j h q", q=QB),
                                   smp_qall[rows, :, :, b * DEC_SEQ:b * DEC_SEQ + QB])
                nc.scalar.copy(smp_eb, smp_e[:, b, :]).then_inc(s_qbd, 1)

            yield AT_S_ATT - 0.02
            queries_of(0)
            for b in range(DEC_BATCH):
                at = AT_S_ATT + b * S_ATT_STEP
                yield at + 0.2 * S_ATT_STEP
                act.wait_ge(s_max, b + 1)
                pieces = ((s_bank[0][:, :], 0), (s_bank[1][:, :], BLK), (t_bank[0][:, 0:DEC_SEQ], 2 * BLK))
                for j, (src, col) in enumerate(pieces):
                    last = nc.scalar.activation(smp_p[:, col:col + src.shape[1]], src, ACT.Exp, bias=smp_stat[:, 4:5],
                                                scale=ATT_SCALE, accum_out=smp_stat[:, 5 + j:6 + j])
                last.then_inc(s_exp, 1)
                if b + 1 < DEC_BATCH:
                    queries_of(b + 1)
                for j, (src, lo, hi) in enumerate(((t_bank[1], 0, 4), (wide[:, 0:BLK], 4, 8))):
                    yield at + (0.42 + 0.05 * j) * S_ATT_STEP
                    act.wait_ge(s_pt, b * 3 + j + 1)
                    if j == 0:
                        act.wait_ge(s_pv, b + 1)
                    nc.scalar.copy(smp_pt[:, lo:hi, :], src[:, :].rearrange("p (t n) -> p t n", t=4)).then_inc(s_ptc, 1)
                act.wait_ge(s_pt, b * 3 + 3)
                nc.scalar.copy(smp_pt[0:DEC_SEQ, 8, :], wide[0:DEC_SEQ, BLK:BLK + P]).then_inc(s_ptc, 1)
            yield from tail(S_T, n)

        def hand_over(u, v, n=SLOTS, total=None):
            if v is not None:
                act.wait_ge(dotted, v * SLOTS + SLOTS + RING if total is None else total)
                nc.scalar.activation(gelu_a[:, 0:n], dots[:, 0:n], ACT.Gelu).then_inc(gelued, 1)
            if u is not None:
                act.wait_ge(routed, u + 2)
                if v is not None:
                    act.wait_ge(hu_read, v + 1)
                nc.scalar.copy(h_u, h_t).then_inc(hu_ready, 1)
            if v is not None:
                act.wait_ge(weighted, v + 1)

        def diagonals(v, n, lag, m, weights_id):
            for s in range(n):
                if not on_pe(v, s):
                    continue
                yield (s + lag - 1) / N_STEPS
                act.wait_ge(summed, summed_before(v) + (number(v, s) + 1))
                nc.scalar.activation(dg[:, number(v, s) % RING, 0:m], weights_id, ACT.Copy,
                                     scale=w_v[:, s:s + 1]).then_inc(diag_ready, 1)

        def finish(v, n):
            act.wait_ge(var2_ready, v + 1)
            nc.scalar.activation(f_rstd[0:n, :], f_mean_var[0:n, 1:2], ACT.Sqrt).then_inc(std2_ready, 1)

        act.wait_ge(consts_in, 64)
        act.wait_ge(s_zero, 5)
        weave(Strand(front(0)), Strand(store_blocks(1, lambda g: group_at(g + 1.4),
                                                     projected_b, z_copied_b, z_stored_b)))
        hand_over(0, None)
        act.wait_ge(z_stored_b, 16 * N_GROUPS_B)
        weave(Strand(front(1)), Strand(store_blocks(3, lambda g: group_at(g + 1.6 - 0.5 * (g % 2), 0.95),
                                                     projected_c, z_copied_c, z_stored_c)))
        with act.Fori(1, N_TILES - 1) as t:
            hand_over(t, t - 1)
            weave(Strand(front(t + 1)), Strand(diagonals(t - 1, SLOTS, LAG, P, ident[:, :])))
            finish(t - 1, P)
        hand_over(N_TILES - 1, N_TILES - 2)
        sample = Strand(front_sample())
        weave(sample, Strand(diagonals(N_TILES - 2, SLOTS, LAG, P, ident[:, :])), 1.0)
        finish(N_TILES - 2, P)
        hand_over(None, N_TILES - 1)
        weave(sample, Strand(1 + x for x in diagonals(N_TILES - 1, SLOTS, 0, P, ident[:, :])))
        finish(N_TILES - 1, P)
        hand_over(None, S_T, Q_SLOTS, S_T * SLOTS + Q_SLOTS + RING)
        weave(nothing(), Strand(diagonals(S_T, Q_SLOTS, 0, N_SAMPLE, quarter)))
        finish(S_T, N_SAMPLE)

    @block.tensor
    def _(pe):
        def project(i, r, width):
            pe.wait_ge(z_copied, i * 2 + (r + 1))
            for c in range(KC):
                last = nc.tensor.matmul(bank[r][:, 0:width], xT_a[:, c, :], w_ring[:, r, c, 0:width], start=(c == 0),
                                        stop=(c == KC - 1))
            last.then_inc(projected, 1)

        pe.wait_ge(xT_in, 16)
        with pe.Fori(0, N_BLK // 2) as i:
            for r in range(2):
                pe.wait_ge(w_in[r], i * 16 + 16)
                project(i, r, BLK)
        pe.wait_ge(w_in[0], 16 * (N_BLK // 2) + 16)
        project(N_BLK // 2, 0, BLK_REST)

        def project_b():
            pe.wait_ge(xT_b_in, 16)
            for g in range(N_GROUPS_B):
                i, t = g // 2, g % 2
                width = BLK if i < N_BLK else BLK_REST
                yield group_at(g)
                pe.wait_ge(w_in_b[i % 2], 16 * (i // 2) + 16)
                if g >= 2:
                    pe.wait_ge(z_copied_b, g - 1)
                for c in range(KC):
                    if c == KC // 2:
                        yield group_at(g + 0.5)
                    last = nc.tensor.matmul(acc[:, g % 2 * BLK:g % 2 * BLK + width], xT_b[:, c, t * P:(t + 1) * P],
                                            w_ring[:, i % 2, c, 0:width], start=(c == 0), stop=(c == KC - 1))
                last.then_inc(projected_b, 1)

        def project_c():
            for k in range(2 * (N_BLK + 1)):
                i, half = k // 2, k % 2
                width = BLK if i < N_BLK else BLK_REST
                yield group_at(k, 0.95)
                if k == 0:
                    pe.wait_ge(xT_c_in, 32)
                    pe.wait_ge(z_copied_b, N_GROUPS_B)
                pe.wait_ge(w_in_c[half], 16 * i + 16)
                for j, n in enumerate((P, N_SAMPLE)):
                    if j:
                        yield group_at(k + 0.5, 0.95)
                    if half == 0 and i:
                        pe.wait_ge(z_copied_c, 2 * (i - 1) + j + 1)
                    for c in range(KC // 2):
                        last = nc.tensor.matmul(acc[0:n, j * BLK:j * BLK + width], xT_c[j][:, KC // 2 * half + c, :],
                                                w_halves[:, half, c, 0:width], start=(half == 0 and c == 0),
                                                stop=(half == 1 and c == KC // 2 - 1))
                    if half == 1:
                        last.then_inc(projected_c, 1)
                if half == 0:
                    last.then_inc(half_used, 1)

        def transpose_group(dst, parts, n, width):
            for i, part in enumerate(parts):
                last = nc.tensor.transpose(dst[0:width, i * n:(i + 1) * n], part, ident[0:n, 0:n])
            last.then_inc(transposed, 1)

        def product(dst, n, lhs, rhs, chunks, done, lo, hi):
            for half in range(2):
                for c in range(chunks):
                    yield lo + (hi - lo) * (half * chunks + c) / (2 * chunks)
                    last = nc.tensor.matmul(dst[0:n, half * BLK:(half + 1) * BLK], lhs[:, c, 0:n],
                                            rhs[:, c, half * BLK:(half + 1) * BLK], start=(c == 0),
                                            stop=(c == chunks - 1))
            last.then_inc(done, 1)

        def halves(src, n, done):
            for r in range(2):
                for c in range(4):
                    last = nc.tensor.transpose(t_bank[r][:, c * P:c * P + n], src[0:n, (4 * r + c) * P:(4 * r + c + 1) * P],
                                               ident[0:n, 0:n])
                last.then_inc(done, 1)

        def conv(t, n):
            yield conv_at(0.482, n)
            pe.wait_ge(conv_done, t + 1)
            for c in range(CC):
                last = nc.tensor.transpose(t_bank[0][0:n, c * P:(c + 1) * P],
                                           ca3[:, c, :] if n == P else smp_acc[:, c, :], ident[:, :])
            last.then_inc(conv_t, 1)
            yield conv_at(0.497, n)
            pe.wait_ge(conv_normed, t + 1)
            for c in range(CC):
                last = nc.tensor.transpose(t_bank[1][:, c * P:c * P + n], conv_n[0:n, c * P:(c + 1) * P],
                                           ident[0:n, 0:n])
            last.then_inc(conv_t2, 1)
            yield conv_at(0.507, n)
            pe.wait_ge(conv_act, t + 1)
            if n == P:
                pe.wait_ge(att_ready, t + 1)
            else:
                pe.wait_ge(s_summed_out, 1)
            if isinstance(t, int) and t == 0:
                pe.wait_ge(weights_in, 64)
            yield from product(wide, n, cy3, wco, CC, conv_mm, conv_at(0.51, n), conv_at(0.537, n))

        def tail(t, n):
            yield tail_at(0.549, n)
            pe.wait_ge(merged, t + 1)
            halves(zt[:, Z_GC:Z_GC + D_MODEL], n, m_trans)
            yield tail_at(0.558, n)
            pe.wait_ge(m_copied, 2 * t + 2)
            yield from product(wide, n, aT3, wou, KC, out_mm, tail_at(0.56, n), tail_at(0.618, n))
            yield tail_at(0.638, n)
            pe.wait_ge(h_ready, t + 1)
            halves(h_t, n, h_trans)
            yield tail_at(0.648, n)
            pe.wait_ge(h_copied, 2 * t + 2)
            if n == N_SAMPLE:
                pe.wait_ge(w_query_in, 16)
            for r in range(2):
                for h in range(4):
                    yield tail_at(0.65 + 0.006 * (4 * r + h), n)
                    for c in range(KC):
                        col = (4 * r + h) * PEER_DQ
                        last = nc.tensor.matmul(s_bank[r][:, h * P:h * P + n], wqu[:, c, col:col + PEER_DQ],
                                                aT3[:, c, 0:n], start=(c == 0), stop=(c == KC - 1))
                last.then_inc(pq_mm, 1)
            yield tail_at(0.70, n)
            pe.wait_ge(pq_copied, 2 * t + 2)
            for j in range(4):
                rows = slice(64 * (j % 2), 64 * (j % 2) + 64)
                for i in range(4):
                    hd = 4 * (j // 2) + i
                    last = nc.tensor.matmul(key_bank[j][0:n, i * PEER_NKEYS:(i + 1) * PEER_NKEYS], qhT[rows, hd, 0:n],
                                            pk[rows, hd, :], start=True, stop=True)
                last.then_inc(key_mm, 1)

        def front(t):
            here = t * GROUPS
            heads = lambda col, k: [zt[:, col + HEAD_DIM * (4 * k + i):col + HEAD_DIM * (4 * k + i + 1)] for i in range(4)]
            yield 0.02
            wait_apart(pe, roped, t + 1)
            transpose_group(t_bank[0], heads(Z_K, 0), P, HEAD_DIM)
            transpose_group(t_bank[1], [zt[:, Z_KI:Z_KI + IDX_DIM]], P, IDX_DIM)
            for g in range(2):
                yield 0.028
                wait_apart(pe, t_copied, here + 1 + g)
                transpose_group(t_bank[g % 2], heads(Z_QI, g), P, IDX_DIM)
            for g in range(4):
                yield 0.034 + 0.002 * g
                wait_apart(pe, t_copied, here + 3 + g)
                transpose_group(t_bank[g % 2], heads(Z_Q, g), P, HEAD_DIM)
            yield 0.043
            wait_apart(pe, t_copied, here + 7)
            transpose_group(t_bank[0], [zt[:, Z_A + P * c:Z_A + P * (c + 1)] for c in range(CC)], P, P)
            for h in range(IDX_HEADS):
                yield AT_IDX + 0.005 * h
                if h >= 2:
                    pe.wait_ge(idx_relu, t * IDX_HEADS + h - 1)
                nc.tensor.matmul(s_bank[h % 2][:, :], qiT3[:, h, :], kiT[0:IDX_DIM, :], start=True,
                                 stop=True).then_inc(idx_mm, 1)
            yield AT_TOPK
            pe.wait_ge(t_copied, here + 9)
            pe.wait_ge(idx_relu, t * IDX_HEADS + IDX_HEADS)

            def scores(h):
                if h >= 2:
                    pe.wait_ge(maxed, t * N_HEADS + h - 1)
                nc.tensor.matmul(s_bank[h % 2][:, :], qT3[:, h, :], kT3[:, HEAD_AT[h] // KV_GROUP, :], start=True,
                                 stop=True).then_inc(qk_mm, 1)

            scores(0)
            scores(1)
            yield AT_ATT + 0.5 * HEAD_STEP
            pe.wait_ge(v_kept, t + 1)
            for h in range(N_HEADS):
                yield AT_ATT + (h + 0.9) * HEAD_STEP
                wait_apart(pe, exped, t * N_HEADS + h + 1)
                if h >= 2:
                    pe.wait_ge(p_copied, t * N_HEADS + h - 1)
                for j in range(N_TILES):
                    last = nc.tensor.transpose(t_bank[h % 2][:, j * P:(j + 1) * P], sc2[:, h % 2, j * P:(j + 1) * P],
                                               ident[:, :])
                last.then_inc(p_trans, 1)
                if h + 2 < N_HEADS:
                    scores(h + 2)
                yield AT_ATT + (h + 1.2) * HEAD_STEP
                pe.wait_ge(p_copied, t * N_HEADS + h + 1)
                for j in range(N_TILES):
                    o, g = HEAD_AT[h], HEAD_AT[h] // KV_GROUP
                    last = nc.tensor.matmul(wide[:, o * HEAD_DIM:(o + 1) * HEAD_DIM], pt2[:, h % 2, j * P:(j + 1) * P],
                                            v3[:, j, g * HEAD_DIM:(g + 1) * HEAD_DIM], start=(j == 0),
                                            stop=(j == N_TILES - 1))
                last.then_inc(pv_mm, 1)
            yield from conv(t, P)
            yield from tail(t, P)

        def front_sample():
            n = N_SAMPLE
            base = N_TILES * GROUPS
            yield 0.02
            pe.wait_ge(roped, S_T + 1)
            transpose_group(t_bank[0], [zt[0:n, Z_K + P * j:Z_K + P * (j + 1)] for j in range(2)], n, P)
            transpose_group(t_bank[1], [zt[0:n, Z_KI:Z_KI + IDX_DIM]], n, IDX_DIM)
            yield 0.028
            pe.wait_ge(t_copied, base + 1)
            transpose_group(t_bank[0], [zt[0:n, Z_QI + IDX_DIM * h:Z_QI + IDX_DIM * (h + 1)] for h in range(IDX_HEADS)],
                            n, IDX_DIM)
            pe.wait_ge(t_copied, base + 2)
            transpose_group(t_bank[1], [zt[0:n, Z_Q + P * j:Z_Q + P * (j + 1)] for j in range(8)], n, P)
            yield 0.034
            pe.wait_ge(t_copied, base + 3)
            transpose_group(t_bank[0], [zt[0:n, Z_A + P * c:Z_A + P * (c + 1)] for c in range(CC)], n, P)
            yield 0.04
            pe.wait_ge(t_copied, base + 5)
            spans = ((s_bank[0], wide[:, 0:BLK], 0, BLK), (s_bank[1], wide[:, BLK:], BLK, BLK),
                     (t_bank[0], t_bank[1], 2 * BLK, DEC_SEQ))
            for _, dst, col, width in spans:
                start_from = (zero[0:n, 0:n], wou[0:n, 0, 0:BLK]) if width == BLK else (ident[0:n, 0:n], smp_causal)
                nc.tensor.matmul(dst[0:n, 0:width], *start_from, start=True, stop=False, skip_group_check=True)
            for b in range(DEC_BATCH):
                new = slice(b * DEC_SEQ, (b + 1) * DEC_SEQ)
                yield AT_S_SUM + (b + 0.1) * S_IDX_STEP
                pe.wait_ge(s_idx_relu, b + 1)
                pe.wait_ge(kidx_in[b % 2], 128 * (b // 2) + 128)
                pe.wait_ge(s_new, b + 1)
                for src, _, col, width in spans:
                    last = nc.tensor.matmul(src[0:n, 0:width], smp_qi[b % 2].rearrange("p h q -> p (h q)"),
                                            smp_ki[b % 2][:, col:col + width] if width == BLK else smp_kinew[:, new],
                                            start=True, stop=True)
                last.then_inc(s_idx_mm, 1)
                yield AT_S_SUM + (b + 0.5) * S_IDX_STEP
                pe.wait_ge(s_idx_relu, b + 2)
                pe.wait_ge(s_wsel, b + 1)
                for _, dst, col, width in spans:
                    last = nc.tensor.matmul(dst[0:n, 0:width], smp_wb[b % 2], smp_relu[:, col:col + width], start=False,
                                            stop=False, skip_group_check=True)
                last.then_inc(s_idx_sum, 1)

            yield from conv(S_T, n)

            def scores(b, at, step):
                pe.wait_ge(k_in[b % 2], 128 * (b // 2) + 128)
                pe.wait_ge(s_qbd, b + 1)
                for i, (dst, _, col, width) in enumerate(spans):
                    if i:
                        yield at + step * i
                    nc.tensor.matmul(dst[:, 0:width], smp_eb, smp_score[:, col:col + width], start=True, stop=False,
                                     skip_group_check=True)
                    for j in range(2):
                        keys = smp_k[b % 2][:, j, col:col + width] if width == BLK else \
                            smp_knew[:, j, b * DEC_SEQ:(b + 1) * DEC_SEQ]
                        last = nc.tensor.matmul(dst[64 * j:64 * j + 64, 0:width], smp_qbd[:, j, :], keys, start=False,
                                                stop=(j == 1), skip_group_check=True)
                last.then_inc(s_qk, 1)

            yield AT_S_ATT - 0.02
            pe.wait_ge(s_bias, 1)
            yield from scores(0, AT_S_ATT - 0.02, 0.005)
            for b in range(DEC_BATCH):
                at = AT_S_ATT + b * S_ATT_STEP
                yield at + 0.4 * S_ATT_STEP
                pe.wait_ge(s_exp, b + 1)
                for dst, lo in ((t_bank[1], 0), (wide, 4)):
                    for j in range(4):
                        last = nc.tensor.transpose(dst[:, j * P:(j + 1) * P], smp_p[:, (lo + j) * P:(lo + j + 1) * P],
                                                   ident[:, :])
                    last.then_inc(s_pt, 1)
                pe.wait_ge(s_o, b + 1)
                nc.tensor.transpose(wide[0:DEC_SEQ, BLK:BLK + P], smp_p[:, PAST_LEN:], ident[:, :]).then_inc(s_pt, 1)
                if b + 1 < DEC_BATCH:
                    yield at + 0.5 * S_ATT_STEP
                    yield from scores(b + 1, at + 0.5 * S_ATT_STEP, 0.15 * S_ATT_STEP)
                yield at + 0.9 * S_ATT_STEP
                pe.wait_ge(s_ptc, b * 3 + 3)
                pe.wait_ge(v_pages_in[b % 2], 128 * (b // 2) + 128)
                pe.wait_ge(vnew_in, 16)
                for j in range(N_PAGES + 1):
                    rows, values = (P, smp_v[b % 2][:, j, :]) if j < N_PAGES else (DEC_SEQ, smp_vnew[:, b, :])
                    last = nc.tensor.matmul(wide[:, BLK:BLK + D_KV], smp_pt[0:rows, j, :], values, start=(j == 0),
                                            stop=(j == N_PAGES))
                last.then_inc(s_pv, 1)
            yield from tail(S_T, n)

        def experts(v, n, lag, m):
            for s in range(n):
                if not on_pe(v, s):
                    continue
                ring, place, landed, value = home(v, s)
                yield (s + lag) / N_STEPS
                if s == 0:
                    pe.wait_ge(acc_taken, v + 1)
                    for half in range(2):
                        nc.tensor.matmul(acc[0:m, half * BLK:(half + 1) * BLK], zero[:, 0:m], wou[:, half, 0:BLK],
                                         start=True, stop=False, skip_group_check=True)
                pe.wait_ge(landed[place], value)
                pe.wait_ge(diag_ready, summed_before(v) + (number(v, s) + 1))
                for half in range(2):
                    last = nc.tensor.matmul(acc[0:m, half * BLK:(half + 1) * BLK], dg[:, number(v, s) % RING, 0:m],
                                            ring[:, place, half * BLK:(half + 1) * BLK], start=False,
                                            stop=False, skip_group_check=True)
                last.then_inc(summed, 1)

        pe.sem_inc(summed, RING)
        pe.wait_ge(consts_in, 64)
        pe.wait_ge(s_zero, 5)
        weave(Strand(front(0)), Strand(project_b()))
        weave(Strand(front(1)), Strand(project_c()))
        with pe.Fori(1, N_TILES - 1) as t:
            weave(Strand(front(t + 1)), Strand(experts(t - 1, SLOTS, LAG, P)))
        sample = Strand(front_sample())
        weave(sample, Strand(experts(N_TILES - 2, SLOTS, LAG, P)), 1.0)
        weave(sample, Strand(1 + x for x in experts(N_TILES - 1, SLOTS, 0, P)))
        weave(nothing(), Strand(experts(S_T, Q_SLOTS, 0, N_SAMPLE)))

    @block.vector
    def _(dve):
        chain = Chain(dve, dve_chain)
        V = nc.vector

        def rotate(t, n):
            dve.wait_ge(z_loaded, 48 * t + 48)
            dve.wait_ge(sig_b, t + 1)
            V.tensor_tensor(zt[0:n, Z_A:Z_A + D_CONV], zt[0:n, Z_A:Z_A + D_CONV], zt[0:n, Z_B:Z_B + D_CONV],
                            ALU.mult).then_inc(u_ready, 1)
            x = zt[0:n, Z_Q:Z_V].rearrange("p (h d) -> p h d", d=HEAD_DIM)[:, :, 0:ROPE_DIM]
            half = ROPE_DIM // 2
            with_cos = rope_tmp[0:n, 0:N_ROT * ROPE_DIM].rearrange("p (h d) -> p h d", d=ROPE_DIM)
            with_sin = rope_tmp[0:n, N_ROT * ROPE_DIM:].rearrange("p (h d) -> p h d", d=ROPE_DIM)
            cos = rope[0:n, 0:ROPE_DIM].unsqueeze(1).to_broadcast([n, N_ROT, ROPE_DIM])
            sin = [rope[0:n, ROPE_DIM + half * k:ROPE_DIM + half * (k + 1)].unsqueeze(1).to_broadcast([n, N_ROT, half])
                   for k in range(2)]
            V.tensor_tensor(with_cos, x, cos, ALU.mult)
            V.tensor_tensor(with_sin[:, :, 0:half], x[:, :, half:], sin[0], ALU.mult)
            chain.link(V.tensor_tensor(with_sin[:, :, half:], x[:, :, 0:half], sin[1], ALU.mult))
            V.tensor_tensor(x, with_cos, with_sin, ALU.add).then_inc(roped, 1)

        def take_top(values, rounds, lo, hi):
            top = top8[0:values.shape[0], :]
            for k in range(rounds):
                yield lo + (hi - lo) * k / rounds
                chain.link(V.max(top, values))
                if k % 2 == 0 and values.shape[1] > BLK:
                    yield lo + (hi - lo) * (k + 0.5) / rounds
                chain.link(V.match_replace(values, top, values, TAKEN))

        def norm(dst, src, n, width, number, second=False):
            st, mv, rs = (f_stats, f_mean_var, f_rstd) if second else (stats, mean_var, rstd)
            k = width // BLK
            for i in range(k):
                m = chain.mark(V.bn_stats(st[0:n, 6 * i:6 * i + 6], src[0:n, i * BLK:(i + 1) * BLK]))
            chain.until(m)
            chain.link(V.bn_aggr(mv[0:n, :], st[0:n, 0:6 * k]))
            V.tensor_scalar(mv[0:n, 1:2], mv[0:n, 1:2], LN_EPS, None,
                            ALU.add).then_inc(var2_ready if second else var_ready, 1)
            dve.wait_ge(std2_ready if second else std_ready, number + 1)
            chain.link(V.reciprocal(rs[0:n, :], rs[0:n, :]))
            return V.tensor_scalar(dst[0:n, :], src[0:n, 0:width], mv[0:n, 0:1], rs[0:n, :], ALU.subtract, ALU.mult)

        def conv(t, n):
            yield conv_at(0.485, n)
            dve.wait_ge(conv_t, t + 1)
            norm(conv_n, t_bank[0], n, D_CONV, 2 * t).then_inc(conv_normed, 1)
            yield conv_at(0.54, n)
            dve.wait_ge(gates_ready, t + 1)
            dve.wait_ge(conv_mm, t + 1)
            gc = zt[0:n, Z_GC:Z_GC + D_MODEL]
            chain.link(V.tensor_tensor(gc, gc, wide[0:n, :], ALU.mult))

        def tail(t, n):
            att, gc, ga = (zt[0:n, z:z + D_MODEL] for z in (Z_Q, Z_GC, Z_GA))
            yield tail_at(0.541, n)
            chain.link(V.tensor_tensor(ga, ga, att, ALU.mult))
            V.tensor_tensor(gc, gc, ga, ALU.add).then_inc(merged, 1)
            yield tail_at(0.62, n)
            dve.wait_ge(out_mm, t + 1)
            dve.wait_ge(x_in, 32 * t + 32)
            h = h_t[0:n, :]
            chain.link(V.scalar_tensor_tensor(h, h, ALPHA, wide[0:n, :], ALU.mult, ALU.add))
            chain.link(norm(h_t, h_t, n, D_MODEL, 2 * t + 1))
            yield tail_at(0.63, n)
            chain.link(V.tensor_tensor(h, h, ln_gb[0:n, 0, :], ALU.mult))
            V.tensor_tensor(h, h, ln_gb[0:n, 1, :], ALU.add).then_inc(h_ready, 1)
            yield tail_at(AT_PEER, n)
            wait_apart(dve, key_copied, 4 * t + 4)
            for hd in range(PEER_HEADS):
                for side in range(2):
                    yield tail_at(AT_PEER + 0.0075 * (2 * hd + side), n)
                    s, tv, ti = sk[0:n, hd, side, :], top_v[0:n, hd, side, :], top_i[0:n, hd, side, :]
                    chain.link(V.max(tv[:, 0:8], s))
                    chain.mark(V.max_index(ti[:, 0:8], tv[:, 0:8], s))
                    chain.link(V.match_replace(s, tv[:, 0:8], s, TAKEN))
                    chain.link(V.max(tv[:, 8:16], s))
                    m = chain.mark(V.max_index(ti[:, 8:16], tv[:, 8:16], s))
            chain.until(m)
            yield tail_at(0.83, n)
            chain.mark(V.tensor_copy(top_if[0:n], top_i[0:n]))
            chain.link(V.tensor_tensor(
                cand[0:n].rearrange("p h (i j) -> p h i j", i=PEER_TOPK),
                top_v[0:n, :, 0, :].unsqueeze(3).to_broadcast([n, PEER_HEADS, PEER_TOPK, PEER_TOPK]),
                top_v[0:n, :, 1, :].unsqueeze(2).to_broadcast([n, PEER_HEADS, PEER_TOPK, PEER_TOPK]), ALU.add))
            for hd in range(PEER_HEADS):
                yield tail_at(0.84 + 0.01 * hd, n)
                s, lo = cand[0:n, hd, :], PEER_TOPK * hd
                chain.link(V.max(c_val[0:n, lo:lo + 8], s))
                chain.mark(V.max_index(c_idx[0:n, lo:lo + 8], c_val[0:n, lo:lo + 8], s))
                chain.link(V.match_replace(s, c_val[0:n, lo:lo + 8], s, TAKEN))
                chain.link(V.max(c_val[0:n, lo + 8:lo + 16], s))
                m = chain.mark(V.max_index(c_idx[0:n, lo + 8:lo + 16], c_val[0:n, lo + 8:lo + 16], s))
            chain.until(m)
            yield tail_at(0.92, n)
            val3 = c_val[0:n, :].rearrange("p (h k) -> p h k", h=PEER_HEADS)
            V.tensor_tensor(logits[0:n, :].rearrange("p (h k) -> p h k", h=PEER_HEADS), val3,
                            val3[:, :, 0:1].to_broadcast([n, PEER_HEADS, PEER_TOPK]),
                            ALU.subtract).then_inc(logits_ready, 1)
            for side, found in ((0, c_e1), (1, c_e2)):
                if side == 0:
                    chain.link(V.tensor_scalar(c_rowu[0:n, :], c_idx[0:n, :], 4, None, ALU.logical_shift_right))
                else:
                    chain.link(V.tensor_scalar(c_rowu[0:n, :], c_idx[0:n, :], 15, None, ALU.bitwise_and))
                chain.link(V.tensor_copy(c_row[0:n, :], c_rowu[0:n, :]))
                yield tail_at(0.93 + 0.03 * side, n)
                chain.link(V.tensor_tensor(onehot[0:n], c_row[0:n, :].unsqueeze(2).to_broadcast([n, SLOTS, PEER_TOPK]),
                                           iota16[0:n, :].unsqueeze(1).to_broadcast([n, SLOTS, PEER_TOPK]),
                                           ALU.is_equal))
                oh4 = onehot[0:n].rearrange("p (h k) j -> p h k j", h=PEER_HEADS)
                yield tail_at(0.94 + 0.03 * side, n)
                chain.link(V.tensor_tensor(
                    oh4, oh4, top_if[0:n, :, side, :].unsqueeze(2).to_broadcast([n, PEER_HEADS, PEER_TOPK, PEER_TOPK]),
                    ALU.mult))
                yield tail_at(0.95 + 0.03 * side, n)
                chain.link(V.tensor_reduce(found[0:n, :], onehot[0:n], AX.X, ALU.add))
            chain.link(V.scalar_tensor_tensor(c_row[0:n, :], c_e1[0:n, :], float(PEER_NKEYS), c_e2[0:n, :], ALU.mult,
                                              ALU.add))
            dve.wait_ge(eu_ready, t + 1)
            chain.mark(V.tensor_copy(eidx[0:n, :], c_row[0:n, :]))
            dve.wait_ge(exp_ready, t + 1)
            g3 = gate[0:n, :].rearrange("p (h k) -> p h k", h=PEER_HEADS)
            chain.link(V.tensor_reduce(g_sum[0:n, :], g3, AX.X, ALU.add))
            chain.link(V.reciprocal(g_inv[0:n, :], g_sum[0:n, :]))
            V.tensor_tensor(g3, g3, g_inv[0:n, :].unsqueeze(2).to_broadcast([n, PEER_HEADS, PEER_TOPK]),
                            ALU.mult).then_inc(routed, 1)

        def front(t):
            yield 0.0
            rotate(t, P)
            yield AT_IDX
            chain.link(V.tensor_scalar(wi_s[:, :], zt[:, Z_WI:Z_WI + IDX_HEADS], IDX_SCALE, None, ALU.mult))
            for h in range(IDX_HEADS):
                yield AT_IDX + 0.005 * h + 0.002
                dve.wait_ge(idx_relu, t * IDX_HEADS + h + 1)
                V.scalar_tensor_tensor(score[:, :], sc2[:, h % 2, :], wi_s[:, h:h + 1],
                                       causal[:, :] if h == 0 else score[:, :], ALU.mult, ALU.add).then_inc(idx_used, 1)
                wait_apart(dve, idx_used, t * IDX_HEADS + h + 1)
            yield from take_top(score, TOPK_PROMPT // 8, AT_TOPK + 0.005, AT_ATT - 0.01)
            chain.link(V.tensor_scalar(bias[:, :], score[:, :], TAKEN_LIMIT, MASKED, ALU.is_gt, ALU.mult))
            chain.link(V.tensor_tensor(bias[:, :], bias[:, :], causal[:, :], ALU.add))

            def tap(k):
                for c in range(CC):
                    src = uT3[:, c, k:k + P]
                    if k == 0:
                        ins = V.tensor_scalar(ca3[:, c, :], src, cp[:, c, 0:1], cp[:, c, CONV_W:CONV_W + 1], ALU.mult,
                                              ALU.add)
                    else:
                        chain.until(tapped[c])
                        ins = V.scalar_tensor_tensor(ca3[:, c, :], src, cp[:, c, k:k + 1], ca3[:, c, :], ALU.mult,
                                                     ALU.add)
                    tapped[c] = chain.mark(ins)

            tapped = [0] * CC
            for h in range(N_HEADS):
                yield AT_ATT + (h - 0.5) * HEAD_STEP
                if h >= 2:
                    dve.wait_ge(p_trans, t * N_HEADS + h - 1)
                wait_apart(dve, qk_mm, t * N_HEADS + h + 1)
                chain.link(V.tensor_tensor_reduce(out=sc2[:, h % 2, :], in0=s_bank[h % 2][:, :], in1=bias[:, :],
                                                  scale=1.0, scalar=TAKEN, op0=ALU.add, op1=ALU.max,
                                                  accum_out=row_max[:, h:h + 1]))
                V.tensor_scalar(neg_max[:, h:h + 1], row_max[:, h:h + 1], -ATT_SCALE, None,
                                ALU.mult).then_inc(maxed, 1)
                if h == 0:
                    dve.wait_ge(t_copied, t * GROUPS + GROUPS)
                for k in range(2 * h, min(2 * h + 2, CONV_W)):
                    yield AT_ATT + (h - 0.4 + 0.4 * (k % 2)) * HEAD_STEP
                    tap(k)
            chain.until(max(tapped))
            V.nop().then_inc(conv_done, 1)
            yield AT_TAIL + 0.001
            dve.wait_ge(pv_mm, t * N_HEADS + N_HEADS)
            chain.link(V.reciprocal(row_inv[:, :], row_sum[:, :]))
            V.tensor_tensor(zt[:, Z_Q:Z_Q + D_MODEL].rearrange("p (h d) -> p h d", h=N_HEADS),
                            wide[:, :].rearrange("p (h d) -> p h d", h=N_HEADS),
                            row_inv[:, :].unsqueeze(2).to_broadcast([P, N_HEADS, HEAD_DIM]),
                            ALU.mult).then_inc(att_ready, 1)
            yield from conv(t, P)
            yield from tail(t, P)

        def front_sample():
            n = N_SAMPLE
            yield 0.0
            rotate(S_T, n)
            yield 0.04
            dve.wait_ge(page_in, 16 * 11)
            dve.wait_ge(t_copied, N_TILES * GROUPS + 5)

            def weights_of(b):
                dve.wait_ge(s_idx_sum, b + 1)
                V.tensor_scalar(smp_wb[b % 2], smp_sel[:, b, :], smp_wi[:, b:b + 1], IDX_SCALE, ALU.mult,
                                ALU.mult).then_inc(s_wsel, 1)

            m = [0] * CC
            for k in range(CONV_W):
                if k % 4 == 0:
                    yield AT_S_SUM + k // 4 * S_IDX_STEP
                    weights_of(k // 4)
                elif k % 2 == 0:
                    yield AT_S_SUM + k / 4 * S_IDX_STEP
                for c in range(CC):
                    src, dst = smp_uT[:, c, :, k:k + DEC_SEQ], smp_acc3[:, c]
                    if k == 0:
                        ins = V.tensor_scalar(dst, src, cp[:, c, 0:1], cp[:, c, CONV_W:CONV_W + 1], ALU.mult, ALU.add)
                    else:
                        chain.until(m[c])
                        ins = V.scalar_tensor_tensor(dst, src, cp[:, c, k:k + 1], dst, ALU.mult, ALU.add)
                    m[c] = chain.mark(ins)
            chain.until(max(m))
            V.nop().then_inc(conv_done, 1)
            yield AT_S_TOPK
            dve.wait_ge(s_idx_sum, DEC_BATCH + 2)
            chain.mark(V.tensor_copy(smp_score[:, 0:2 * BLK], wide[0:n, :]))
            chain.link(V.tensor_copy(smp_score[:, 2 * BLK:], t_bank[1][0:n, 0:DEC_SEQ]))
            V.nop().then_inc(s_summed_out, 1)
            yield from merge(Strand(conv(S_T, n)),
                             Strand(take_top(smp_score, TOPK_SAMPLE // 8, AT_S_TOPK + 0.001, AT_S_ATT - 0.02)))
            chain.link(V.tensor_scalar(smp_score, smp_score, TAKEN_LIMIT, MASKED, ALU.is_gt, ALU.mult))
            new = smp_score[:, PAST_LEN:]
            V.tensor_tensor(new, new, smp_causal, ALU.add).then_inc(s_bias, 1)

            def maximum(b):
                dve.wait_ge(s_qk, b + 1)
                V.tensor_reduce(smp_stat[:, 0:1], s_bank[0][:, :], AX.X, ALU.max)
                V.tensor_reduce(smp_stat[:, 1:2], s_bank[1][:, :], AX.X, ALU.max)
                chain.link(V.tensor_reduce(smp_stat[:, 2:3], t_bank[0][:, 0:DEC_SEQ], AX.X, ALU.max))
                chain.link(V.tensor_reduce(smp_stat[:, 3:4], smp_stat[:, 0:3], AX.X, ALU.max))
                V.tensor_scalar(smp_stat[:, 4:5], smp_stat[:, 3:4], -ATT_SCALE, None, ALU.mult).then_inc(s_max, 1)

            yield AT_S_ATT
            maximum(0)
            for b in range(DEC_BATCH):
                yield AT_S_ATT + (b + 0.5) * S_ATT_STEP
                dve.wait_ge(s_exp, b + 1)
                chain.link(V.tensor_reduce(smp_stat[:, 8:9], smp_stat[:, 5:8], AX.X, ALU.add))
                chain.link(V.reciprocal(smp_stat[:, 9:10], smp_stat[:, 8:9]))
                yield AT_S_ATT + (b + 1.0) * S_ATT_STEP
                if b + 1 < DEC_BATCH:
                    maximum(b + 1)
                    yield AT_S_ATT + (b + 1.1) * S_ATT_STEP
                dve.wait_ge(s_pv, b + 2)
                dve.wait_ge(s_rows, 16 * b + 16)
                for g in range(N_KV):
                    rows = slice(32 * g, 32 * g + 32)
                    last = V.tensor_scalar(smp_o[rows, :], wide[rows, BLK + g * HEAD_DIM:BLK + (g + 1) * HEAD_DIM],
                                           smp_stat[rows, 9:10], None, ALU.mult)
                last.then_inc(s_o, 1)
            yield AT_S_TAIL
            dve.wait_ge(scratch_in, 16 * DEC_BATCH)
            yield from tail(S_T, n)

        def keep_h(v, m):
            V.tensor_scalar(y_v[0:m, :], h_u[0:m, :], ALPHA, None, ALU.mult).then_inc(hu_read, 1)

        def weigh(v, n):
            dve.wait_ge(gelued, v + 1)
            if not (isinstance(v, int) and v == S_T):
                dve.wait_ge(gu_ready, v + 2)
            dve.wait_ge(summed, summed_before(v) + RING)
            V.tensor_tensor(w_v[:, 0:n], gelu_a[:, 0:n], g_u[:, 0:n], ALU.mult).then_inc(weighted, 1)

        def products(u, n):
            for s in range(n):
                yield s / N_STEPS
                if s == 0 and not (isinstance(u, int) and u == S_T):
                    dve.wait_ge(hu_ready, u + 2)
                odd_rows = PER_TILE // 2 if is_tile(u, S_T) else 0
                dve.wait_ge(u_in[s % RING], u * PER_TILE + (s // RING * 16 + 16 + odd_rows))
                V.tensor_tensor_reduce(out=u_ring[:, s % RING, :], in0=u_ring[:, s % RING, :], in1=h_u, scale=1.0,
                                       scalar=0.0, op0=ALU.mult, op1=ALU.add,
                                       accum_out=dots[:, s:s + 1]).then_inc(dotted, 1)

        def sums(v, lag):
            dve.wait_ge(hu_read, v + 1)
            dve.wait_ge(weighted, v + 1)
            for s in range(SLOTS):
                if on_pe(v, s):
                    continue
                ring, place, landed, value = home(v, s)
                yield (s + lag) / N_STEPS
                dve.wait_ge(landed[place], value)
                dve.wait_ge(added, added_before(v) + number(v, s) + 1)
                V.scalar_tensor_tensor(y_v, ring[:, place, :], w_v[:, s:s + 1], y_v, ALU.mult,
                                       ALU.add).then_inc(added, 1)

        def merge(*strands):
            while any(x.at is not None for x in strands):
                x = min((x for x in strands if x.at is not None), key=lambda x: x.at)
                yield x.at
                x.step()

        def finish(v, n, total):
            y = v_ring[0:n, 2, :]
            chain.restart()
            if is_tile(v, LAST - 1, LAST):
                dve.wait_ge(added, added_before(v + 1) + 1)
            dve.wait_ge(summed, total)
            V.tensor_tensor(y, y_v[0:n, :], acc[0:n, :], ALU.add).then_inc(acc_taken, 1)
            wait_apart(dve, acc_taken, v + 2)
            chain.link(norm(v_ring[:, 2, :], v_ring[:, 2, :], n, D_MODEL, v, True))
            dve.wait_ge(ln2_in, 16 * v + 16)
            chain.link(V.tensor_tensor(y, y, v_ring[0:n, 0, :], ALU.mult))
            V.tensor_tensor(y, y, v_ring[0:n, 1, :], ALU.add).then_inc(y_ready, 1)
            chain.restart()

        dve.sem_inc(dotted, RING)
        dve.sem_inc(added, 1)
        dve.sem_inc(acc_taken, 1)
        dve.sem_inc(routed, 1)
        dve.wait_ge(consts_in, 64)
        weave(Strand(front(0)), nothing())
        chain.restart()
        weave(Strand(front(1)), Strand(products(0, SLOTS)))
        dve.wait_ge(projected_c, N_GROUPS_B)
        chain.restart()
        with dve.Fori(1, N_TILES - 1) as t:
            keep_h(t - 1, P)
            weigh(t - 1, SLOTS)
            weave(Strand(front(t + 1)), Strand(products(t, SLOTS)))
            finish(t - 1, P, summed_before(t) + RING)
        keep_h(N_TILES - 2, P)
        weigh(N_TILES - 2, SLOTS)
        sample = Strand(front_sample())
        weave(sample, Strand(merge(Strand(products(LAST, SLOTS)), Strand(sums(LAST - 1, LAG)))), 1.0)
        finish(N_TILES - 2, P, summed_before(N_TILES - 1) + RING)
        keep_h(N_TILES - 1, P)
        weigh(N_TILES - 1, SLOTS)
        weave(sample, Strand(1 + x for x in sums(LAST, 0)))
        finish(N_TILES - 1, P, summed_before(S_T) + RING)
        dve.wait_ge(scratch_in, 16 * 20)
        weave(nothing(), Strand(products(S_T, Q_SLOTS)))
        keep_h(S_T, N_SAMPLE)
        weigh(S_T, Q_SLOTS)
        finish(S_T, N_SAMPLE, summed_before(S_T) + Q_SLOTS + RING)


def _rope_tables():
    half = ROPE_DIM // 2
    inv = np.power(np.float32(ROPE_THETA), -np.arange(half, dtype=np.float32) / np.float32(half)).astype(np.float32)
    pos = np.zeros((N_TILES + 1, P), np.float32)
    pos[:N_TILES] = np.arange(SEQ).reshape(N_TILES, P)
    pos[N_TILES, :N_SAMPLE] = PAST_LEN + np.arange(N_SAMPLE) % DEC_SEQ
    angle = (pos[:, :, None] * inv).astype(np.float32)
    cos, sin = np.cos(angle), np.sin(angle)
    return np.concatenate([cos, cos, -sin, sin], -1).astype(np.float32)


def kernel(**inputs):
    import concourse.bacc as bacc
    from concourse.bass_utils import run_bass_kernel_spmd

    a = {k: np.asarray(v) for k, v in inputs.items()}
    f = np.float32

    def chunks(w):
        c = w.shape[0] // P
        return np.ascontiguousarray(w.reshape(c, P, -1).transpose(1, 0, 2).reshape(P, -1))

    x = np.zeros((N_TILES + 1, P, D_MODEL), f)
    x[:N_TILES] = a["x_prompt"].reshape(N_TILES, P, D_MODEL)
    x[N_TILES, :N_SAMPLE] = a["x_sample"].reshape(N_SAMPLE, D_MODEL)
    tokens = x.reshape(-1, D_MODEL)
    q0 = 2 * D_CONV
    k0 = q0 + N_HEADS * HEAD_DIM
    v0 = k0 + D_KV
    qi0 = v0 + D_KV
    ki0 = qi0 + IDX_HEADS * IDX_DIM
    wi0 = ki0 + IDX_DIM
    w = a["w_in"]
    q_cols = [w[:, q0 + h * HEAD_DIM:q0 + (h + 1) * HEAD_DIM] for h in HEAD_AT]
    w = np.concatenate([w[:, :q0], *q_cols, w[:, k0:v0], w[:, qi0:wi0], w[:, v0:qi0], w[:, wi0:]], 1)
    wb = w[:, :N_BLK * BLK].reshape(KC, P, N_BLK, BLK).transpose(2, 1, 0, 3)
    conv_params = np.concatenate([a["conv_w"], a["conv_b"][None], a["conv_ln_g"][None], a["conv_ln_b"][None]], 0).T
    keys = np.concatenate([a["peer_keys1"].transpose(2, 0, 1), a["peer_keys2"].transpose(2, 0, 1)], 0)
    state = np.zeros((DEC_BATCH, CONV_W - 1 + DEC_SEQ, D_CONV), f)
    state[:, :CONV_W - 1] = a["state_conv"]
    query, key = np.arange(SEQ).reshape(N_TILES, P, 1), np.arange(SEQ)
    causal = np.where(key <= query, f(0), f(MASKED)).astype(f)
    n = np.arange(N_SAMPLE)
    causal_sample = np.where(np.arange(DEC_SEQ)[None] <= (n % DEC_SEQ)[:, None], f(0), f(MASKED)).astype(f)
    batch, row_q = np.arange(DEC_BATCH), np.arange(P) % QB % DEC_SEQ
    spread = (n[:, None, None] == batch[None, :, None] * DEC_SEQ + row_q[None, None, :]).astype(f)
    choose = (n[None, None, :] == batch[None, :, None] * DEC_SEQ + (n % DEC_SEQ)[:, None, None]).astype(f)

    def tokens_T(lo, hi):
        return chunks(np.ascontiguousarray(tokens[lo:hi].T)).reshape(P, KC, -1)

    arrays = {
        "xT_a": tokens_T(0, P),
        "xT_b": tokens_T(P, 3 * P),
        "xT_c0": tokens_T(3 * P, SEQ),
        "xT_c1": tokens_T(SEQ, SEQ + N_SAMPLE),
        "x_rows": x,
        "w_in": np.ascontiguousarray(wb),
        "w_in_rest": np.ascontiguousarray(w[:, N_BLK * BLK:].reshape(KC, P, -1).transpose(1, 0, 2)),
        "w_conv_out": chunks(a["w_conv_out"]),
        "w_out": chunks(a["w_out"]),
        "w_query": chunks(a["peer_w_query"].reshape(D_MODEL, -1)),
        "peer_keys": np.ascontiguousarray(keys.reshape(P, -1)),
        "conv_params": chunks(np.ascontiguousarray(conv_params)),
        "ln1": np.stack([a["ln1_g"], a["ln1_b"]]),
        "ln2": np.stack([a["ln2_g"], a["ln2_b"]]),
        "rope": _rope_tables(),
        "causal": causal,
        "causal_sample": causal_sample,
        "spread": np.ascontiguousarray(spread.reshape(N_SAMPLE, -1)),
        "choose": np.ascontiguousarray(choose.reshape(N_SAMPLE, -1)),
        "ident": np.eye(P, dtype=f),
        "iota16": np.tile(np.arange(PEER_TOPK, dtype=f), (P, 1)),
        "quarter": np.tile(np.eye(N_SAMPLE, dtype=f), (4, 1)),
        "page_table": a["page_table"].reshape(1, -1),
        "state_T": chunks(np.ascontiguousarray(state.transpose(2, 0, 1).reshape(D_CONV, -1))),
        "state_conv": a["state_conv"],
        "cache_kT": np.ascontiguousarray(
            a["cache_k"].reshape(N_POOL, PAGE, 2, P).transpose(0, 3, 2, 1).reshape(N_POOL, P, -1)),
        "cache_v": a["cache_v"].reshape(N_POOL, PAGE, D_KV),
        "kidx_T": np.ascontiguousarray(a["cache_kidx"].transpose(0, 2, 1)),
        "peer_u": a["peer_u"],
        "peer_v": a["peer_v"],
    }
    outputs = {
        "y_prompt": (N_TILES, P, D_MODEL),
        "y_sample": (N_SAMPLE, D_MODEL),
        "k_prompt": (N_TILES, P, D_KV),
        "v_prompt": (N_TILES, P, D_KV),
        "kidx_prompt": (N_TILES, P, IDX_DIM),
        "conv_prompt": (CONV_W - 1, D_CONV),
        "k_sample": (N_SAMPLE, D_KV),
        "v_sample": (N_SAMPLE, D_KV),
        "kidx_sample": (N_SAMPLE, IDX_DIM),
        "conv_sample": (DEC_BATCH, CONV_W - 1, D_CONV),
    }
    nc = bacc.Bacc("TRN2", target_bir_lowering=False, num_devices=1)
    io = {}
    for name, array in arrays.items():
        io[name] = nc.dram_tensor(name, array.shape, mybir.dt.from_np(array.dtype), kind="ExternalInput").ap()
    for name, shape in outputs.items():
        io[name] = nc.dram_tensor(name, shape, F32, kind="ExternalOutput").ap()
    build(nc, io)
    r = run_bass_kernel_spmd(nc, [arrays], core_ids=[0]).results[0]
    return (
        r["y_prompt"].reshape(1, SEQ, D_MODEL),
        r["y_sample"].reshape(DEC_BATCH, DEC_SEQ, D_MODEL),
        r["k_prompt"].reshape(1, SEQ, N_KV, HEAD_DIM),
        r["v_prompt"].reshape(1, SEQ, N_KV, HEAD_DIM),
        r["kidx_prompt"].reshape(1, SEQ, IDX_DIM),
        r["conv_prompt"].reshape(1, CONV_W - 1, D_CONV),
        r["k_sample"].reshape(DEC_BATCH, DEC_SEQ, N_KV, HEAD_DIM),
        r["v_sample"].reshape(DEC_BATCH, DEC_SEQ, N_KV, HEAD_DIM),
        r["kidx_sample"].reshape(DEC_BATCH, DEC_SEQ, IDX_DIM),
        r["conv_sample"],
    )
```
